# Optimizing a Trainium2 kernel written in Bass

```python
import jax, jax.numpy as jnp
from jax import lax
import numpy as np

D_MODEL = 2048
BATCH = 1
SEQ = 256
DEPTH = 1

CHUNK = 64
Q_BLOCK = 128
PLE_DIM = 256
FOX_HEADS = 8
FOX_HEAD_DIM = D_MODEL // 16
GLA_HEADS = 4
GLA_KEY_DIM = D_MODEL // 16
GLA_VAL_DIM = D_MODEL // 8
GLA_GATE_RANK = 16
GLA_GATE_TAU = 16.0
D_FF = ((8 * D_MODEL // 3 + 255) // 256) * 256
EPS = 1e-6

FOX_W = FOX_HEADS * FOX_HEAD_DIM
GLA_KW = GLA_HEADS * GLA_KEY_DIM
GLA_VW = GLA_HEADS * GLA_VAL_DIM
IN_SPLITS = (FOX_W, FOX_W, FOX_W, FOX_HEADS, GLA_KW, GLA_KW, GLA_VW, GLA_VW, GLA_GATE_RANK)
D_IN = sum(IN_SPLITS)

kernel_name = "hybrid_fox_gla_macaron_ple"

def rms_norm(x, g):
    xf = x.astype(jnp.float32)
    y = xf * lax.rsqrt(jnp.mean(xf * xf, axis=-1, keepdims=True) + EPS)
    return (y * g.astype(jnp.float32)).astype(x.dtype)

def swiglu(x, w_gate, w_up, w_down):
    return (jax.nn.silu(x @ w_gate) * (x @ w_up)) @ w_down

def split_cols(t, sizes):
    out, start = [], 0
    for s in sizes:
        out.append(t[..., start:start + s])
        start += s
    return out

def forgetting_attention(q, k, v, log_f):
    b, s, h, d = q.shape
    nb = s // Q_BLOCK
    f_cum = jnp.cumsum(log_f.astype(jnp.float32), axis=1).transpose(0, 2, 1)
    q_blocks = q.reshape(b, nb, Q_BLOCK, h, d).transpose(1, 0, 2, 3, 4)
    fq_blocks = f_cum.reshape(b, h, nb, Q_BLOCK).transpose(2, 0, 1, 3)
    key_pos = jnp.arange(s)
    scale = d ** -0.5

    def block(args):
        q_i, fq_i, i = args
        logits = jnp.einsum('bqhd,bkhd->bhqk', q_i, k).astype(jnp.float32) * scale
        logits = logits + fq_i[..., :, None] - f_cum[:, :, None, :]
        q_pos = i * Q_BLOCK + jnp.arange(Q_BLOCK)
        causal = key_pos[None, :] <= q_pos[:, None]
        logits = jnp.where(causal, logits, -jnp.inf)
        probs = jax.nn.softmax(logits, axis=-1).astype(v.dtype)
        return jnp.einsum('bhqk,bkhd->bqhd', probs, v)

    out = lax.map(block, (q_blocks, fq_blocks, jnp.arange(nb)))
    return out.transpose(1, 0, 2, 3, 4).reshape(b, s, h * d)

def gla_chunk_causal(q, k, v, log_a):
    b, s, h, dk = q.shape
    dv = v.shape[-1]
    nc = s // CHUNK

    def chunks(t):
        return t.astype(jnp.float32).reshape(b, nc, CHUNK, h, t.shape[-1]).transpose(1, 0, 2, 3, 4)

    qc, kc, vc, ac = chunks(q), chunks(k), chunks(v), chunks(log_a)
    a_cum = jnp.cumsum(ac, axis=2)
    a_tot = a_cum[:, :, -1]
    k_dec = kc * jnp.exp(a_tot[:, :, None] - a_cum)
    qc = qc * (dk ** -0.5)

    def step(state, inp):
        q_c, k_c, v_c, a_c = inp
        state = jnp.exp(a_c)[..., None] * state + jnp.einsum('bchk,bchv->bhkv', k_c, v_c)
        o = jnp.einsum('bchk,bhkv->bchv', q_c, state)
        return state, o

    state0 = jnp.zeros((b, h, dk, dv), jnp.float32)
    _, o = lax.scan(step, state0, (qc, k_dec, vc, a_tot))
    return o.transpose(1, 0, 2, 3, 4).reshape(b, s, h, dv)

def setup_inputs(seed: int = 0) -> dict:
    key = jax.random.key(seed)
    ks = iter(jax.random.split(key, 32))
    f32 = jnp.float32

    def w(shape, fan_in):
        return jax.random.normal(next(ks), (DEPTH,) + shape, f32) * (fan_in ** -0.5)

    def gain(shape):
        return 1.0 + 0.05 * jax.random.normal(next(ks), shape, f32)

    def bias(shape, mean=0.0, std=0.01):
        return mean + std * jax.random.normal(next(ks), shape, f32)

    return {
        "x": jax.random.normal(next(ks), (BATCH, SEQ, D_MODEL), f32),
        "p": jax.random.normal(next(ks), (DEPTH, BATCH, SEQ, PLE_DIM), f32),
        "ffn1_norm": gain((DEPTH, D_MODEL)),
        "ffn1_w_gate": w((D_MODEL, D_FF), D_MODEL),
        "ffn1_w_up": w((D_MODEL, D_FF), D_MODEL),
        "ffn1_w_down": w((D_FF, D_MODEL), D_FF),
        "mix_norm": gain((DEPTH, D_MODEL)),
        "w_in": w((D_MODEL, D_IN), D_MODEL),
        "fox_forget_bias": bias((DEPTH, FOX_HEADS), mean=3.0, std=0.1),
        "gla_gate_up": w((GLA_GATE_RANK, GLA_KW), GLA_GATE_RANK),
        "gla_gate_bias": bias((DEPTH, GLA_KW)),
        "gla_head_norm": gain((DEPTH, GLA_VAL_DIM)),
        "w_branch_fox": w((FOX_W, D_MODEL), FOX_W),
        "w_branch_gla": w((GLA_VW, D_MODEL), GLA_VW),
        "w_merge_gate": w((D_MODEL, 2 * D_MODEL), D_MODEL),
        "b_merge_gate": bias((DEPTH, 2 * D_MODEL)),
        "w_out": w((D_MODEL, D_MODEL), D_MODEL),
        "ffn2_norm": gain((DEPTH, D_MODEL)),
        "ffn2_w_gate": w((D_MODEL, D_FF), D_MODEL),
        "ffn2_w_up": w((D_MODEL, D_FF), D_MODEL),
        "ffn2_w_down": w((D_FF, D_MODEL), D_FF),
        "ple_norm": gain((DEPTH, D_MODEL)),
        "w_ple_proj": w((PLE_DIM, D_MODEL), PLE_DIM),
        "w_ple_gate": w((D_MODEL, D_MODEL), D_MODEL),
        "final_norm": gain((D_MODEL,)),
    }

def reference(x, p, ffn1_norm, ffn1_w_gate, ffn1_w_up, ffn1_w_down, mix_norm, w_in,
              fox_forget_bias, gla_gate_up, gla_gate_bias, gla_head_norm,
              w_branch_fox, w_branch_gla, w_merge_gate, b_merge_gate, w_out,
              ffn2_norm, ffn2_w_gate, ffn2_w_up, ffn2_w_down,
              ple_norm, w_ple_proj, w_ple_gate, final_norm):
    b, s, _ = x.shape
    h = x
    for i in range(DEPTH):
        h = h + 0.5 * swiglu(rms_norm(h, ffn1_norm[i]), ffn1_w_gate[i], ffn1_w_up[i], ffn1_w_down[i])

        u = rms_norm(h, mix_norm[i])
        (fq, fk, fv, f_logit, gq, gk, gv, gr, g_down) = split_cols(u @ w_in[i], IN_SPLITS)

        log_f = jax.nn.log_sigmoid((f_logit + fox_forget_bias[i]).astype(jnp.float32))
        y_fox = forgetting_attention(
            fq.reshape(b, s, FOX_HEADS, FOX_HEAD_DIM),
            fk.reshape(b, s, FOX_HEADS, FOX_HEAD_DIM),
            fv.reshape(b, s, FOX_HEADS, FOX_HEAD_DIM),
            log_f.astype(x.dtype))

        log_a = jax.nn.log_sigmoid((g_down @ gla_gate_up[i] + gla_gate_bias[i]).astype(jnp.float32)) / GLA_GATE_TAU
        o_gla = gla_chunk_causal(
            gq.reshape(b, s, GLA_HEADS, GLA_KEY_DIM),
            gk.reshape(b, s, GLA_HEADS, GLA_KEY_DIM),
            gv.reshape(b, s, GLA_HEADS, GLA_VAL_DIM),
            log_a.reshape(b, s, GLA_HEADS, GLA_KEY_DIM))
        o_gla = rms_norm(o_gla, gla_head_norm[i]).reshape(b, s, GLA_VW).astype(x.dtype)
        y_gla = o_gla * jax.nn.silu(gr)

        gates = jax.nn.sigmoid(u @ w_merge_gate[i] + b_merge_gate[i])
        g_fox, g_gla = gates[..., :D_MODEL], gates[..., D_MODEL:]
        merged = g_fox * (y_fox @ w_branch_fox[i]) + g_gla * (y_gla @ w_branch_gla[i])
        h = h + merged @ w_out[i]

        h = h + 0.5 * swiglu(rms_norm(h, ffn2_norm[i]), ffn2_w_gate[i], ffn2_w_up[i], ffn2_w_down[i])

        ple_gate = jax.nn.sigmoid(rms_norm(h, ple_norm[i]) @ w_ple_gate[i])
        h = h + ple_gate * (p[i].astype(h.dtype) @ w_ple_proj[i])
    return rms_norm(h, final_norm)


_drawn_inputs = setup_inputs


def setup_inputs(seed=0):
    import zlib

    import numpy as np

    out = dict(_drawn_inputs(seed))
    spreads = {}
    factors = {'fox_forget_bias': 43.144,
     'gla_gate_bias': 8.0,
     'gla_head_norm': 4.05,
     'b_merge_gate': 8.0,
     'ffn2_norm': 3.282,
     'ple_norm': 143.998}
    for name, (base, spread) in spreads.items():
        noise = np.random.default_rng([zlib.crc32(name.encode()), seed]).standard_normal(out[name].shape)
        drawn = base * np.exp(spread * noise) if base else spread * noise
        out[name] = __import__('jax').numpy.asarray(drawn.astype(out[name].dtype))
    for name, factor in factors.items():
        out[name] = (out[name] * factor).astype(out[name].dtype)
    return out
```

```python
from contextlib import ExitStack

import concourse.bass as bass
from concourse import mybir

P = 128
F32 = mybir.dt.float32
F32R = mybir.dt.float32r
ALU = mybir.AluOpType
ACT = mybir.ActivationFunctionType
AX_X = mybir.AxisListType.X

TOK = 256
TT = TOK // P
D = 2048
KD = D // P
FF = 5632
HALF_KT = (24, 20)
PLE = 256
HEADS = 8
DH = 128
GH = 4
DK = 128
DV = 256
RANK = 16
TAU = 16.0
CHUNK = 64
EPS = 1e-6
COLS = 512
BK = 2
RING = 4
NEG = -3.0e38

FQ, FK, FV, GQ, GK, GV, GR = 0, 8, 16, 24, 28, 32, 40
SLABS = 48
FLOG = 3 * HEADS * DH
GLA0 = FLOG + HEADS
GDOWN = GLA0 + 2 * GH * DK + 2 * GH * DV
THIN = HEADS + RANK

PHASES = {
    "up1a": (12, 8), "down1a": (4, 12), "up1b": (10, 8), "down1b": (4, 10),
    "project": (12, 8), "merge": (8, 8), "branch": (8, 4), "out": (4, 8),
    "up2a": (12, 8), "down2a": (4, 12), "up2b": (10, 8), "down2b": (4, 10),
    "ple": (8, None),
}
PLE_BLOCKS = (8, 1)
TURNS = {"x": 8, "up1a": 12, "up1b": 10, "down1b": 8, "branch": 8, "out": 8,
         "up2a": 12, "up2b": 10, "down2b": 8, "p": 1}


def starts():
    block, group, b, g = {}, {}, 0, 0
    for name, (n, nb) in PHASES.items():
        block[name], group[name] = b, g
        b += n * nb if nb else (n // 2) * sum(PLE_BLOCKS)
        g += n
    turn, t = {}, 0
    for name, n in TURNS.items():
        turn[name] = t
        t += n
    return block, group, turn, b


def build(nc, x, p, ffn1_norm, ffn1_w_gate, ffn1_w_up, ffn1_w_down, mix_norm, w_in,
          fox_forget_bias, gla_gate_up, gla_gate_bias, gla_head_norm, w_branch_fox, w_branch_gla,
          w_merge_gate, b_merge_gate, w_out, ffn2_norm, ffn2_w_gate, ffn2_w_up, ffn2_w_down,
          ple_norm, w_ple_proj, w_ple_gate, final_norm, out):
    BLOCK, GROUP, TURN, END = starts()
    x_tm = x[0].rearrange("(t p) d -> p t d", p=P)
    out_tm = out[0].rearrange("(t p) d -> p t d", p=P)

    with ExitStack() as ctx:
        def sb(name, shape, dt=F32):
            return ctx.enter_context(nc.sbuf_tensor(name, shape, dt))

        def shared(*views):
            size, made = 0, []
            for name, shape, dt in views:
                with nc.sbuf_tensor(name, shape, dt) as made_one:
                    made.append(made_one)
                n = 4
                for s in shape[1:]:
                    n *= s
                size = max(size, n)
            sb(views[0][0] + "_room", [P, size // 4])
            return made

        def sem(name):
            return ctx.enter_context(nc.semaphore(name))

        h = sb("h", [P, TT, D])
        x_hi, x_lo = sb("x_hi", [P, KD, TOK], F32R), sb("x_lo", [P, KD, TOK], F32R)
        slab_r, slab = shared(("slab_r", [P, SLABS, TOK], F32R), ("slab", [P, SLABS, TT, P], F32))
        gates, y_r = shared(("gates", [P, 8, TT, COLS], F32), ("y_r", [P, 2 * KD, TOK], F32R))
        raw = sb("raw", [P, RING, BK, COLS])
        w_hi, w_lo = sb("w_hi", [P, RING, BK, COLS], F32R), sb("w_lo", [P, RING, BK, COLS], F32R)
        scratch = sb("scratch", [P, TT, COLS])
        ident = sb("ident", [P, P])
        later_in_chunk = sb("later_in_chunk", [P, P])
        up_to = sb("up_to", [P, P])
        ones = sb("ones", [P, P])
        behind = sb("behind", [P, TT, TOK])
        causal = sb("causal", [P, 3 * P])
        in_chunk = sb("in_chunk", [P, 2])
        gains_rows = sb("gains_rows", [4 * KD + 2, P])
        gains = sb("gains", [P, 4 * KD + 2])
        minus_half = sb("minus_half", [P, 2])
        sumsq = sb("sumsq", [P, TT, 4])
        meansq = sb("meansq", [P, TT])
        rstd = sb("rstd", [P, TT])
        merge_bias = sb("merge_bias", [P, 2, COLS])
        forget_bias = sb("forget_bias", [P, HEADS])
        thin_z = sb("thin_z", [P, TT, THIN])
        thin_e = sb("thin_e", [P, TT, HEADS])
        log_f = sb("log_f", [P, TT, HEADS])
        qk_t = sb("qk_t", [P, 2 * TOK])
        masked_log_f = sb("masked_log_f", [P, 2, 3, P])
        probs = sb("probs", [P, 3 * P])
        probs_t = sb("probs_t", [P, 3 * P])
        neg_max, row_sum, row_inv = sb("neg_max", [P, 2]), sb("row_sum", [P, 2]), sb("row_inv", [P, 2])
        gq_t = sb("gq_t", [P, 2, TOK])
        state = sb("state", [P, 2, DV])
        decay = sb("decay", [P, GH * 4])
        gla_sumsq, gla_meansq, gla_rstd = sb("gla_sumsq", [P, 2]), sb("gla_meansq", [P, 2]), sb("gla_rstd", [P, 2])
        log_a = gates[:, 7, :, :]
        thin_flat = gates[:, 6, :, :].rearrange("p t c -> p (t c)")
        thin_raw = thin_flat[:, 0:KD * THIN].rearrange("p (k c) -> p k c", k=KD)
        thin_hi, thin_lo = (y_r[:, at:at + 2, :].rearrange("p a b -> p (a b)")[:, 0:KD * THIN]
                            .rearrange("p (k c) -> p k c", k=KD) for at in (0, 2))
        gate_up = gates[0:RANK + 1, 5, 0, :]
        down_t = gates[0:32, 5, 1, 0:TOK]
        slab_flat = slab[:, :, :, :].rearrange("p s t c -> p (s t c)")
        p_tm = slab_flat[:, 0:TT * PLE].rearrange("p (t c) -> p t c", t=TT)
        final_gain = slab_flat[:, TT * PLE:TT * PLE + D]
        P_HI, P_LO = SLABS - 4, SLABS - 2

        acc = [ctx.enter_context(nc.psum_tensor(f"acc{i}", [P, COLS], F32)) for i in range(4)]
        turn_bank = [ctx.enter_context(nc.psum_tensor(f"turn{i}", [P, COLS], F32)) for i in range(2)]
        fox_bank = [ctx.enter_context(nc.psum_tensor(f"fox{i}", [P, COLS], F32)) for i in range(2)]

        raw_full = [sem(f"raw_full{i}") for i in range(RING)]
        hi_split = sem("hi_split")
        lo_split = sem("lo_split")
        multiplied = sem("multiplied")
        read_out = sem("read_out")
        turned = sem("turned")
        turned_hi = sem("turned_hi")
        turned_lo = sem("turned_lo")
        x_full = [sem(f"x_full{i}") for i in range(4)]
        gains_full = sem("gains_full")
        gains_turned, gains_ready = sem("gains_turned"), sem("gains_ready")
        consts = sem("consts")
        pool_chain = sem("pool_chain")
        silu_done = sem("silu_done")
        sumsq_done = sem("sumsq_done")
        meansq_done, rstd_done = sem("meansq_done"), sem("rstd_done")
        sigmoid_done = sem("sigmoid_done")
        dve_chain = sem("dve_chain")
        act_chain = sem("act_chain")
        thin_full, thin_hi_done, thin_lo_done = sem("thin_full"), sem("thin_hi_done"), sem("thin_lo_done")
        thin_mult, thin_scaled, thin_neg, thin_log = (sem(n) for n in ("thin_mult", "thin_scaled", "thin_neg", "thin_log"))
        log_f_done, down_turned, down_ready = sem("log_f_done"), sem("down_turned"), sem("down_ready")
        decay_mult, decay_log, log_a_done = sem("decay_mult"), sem("decay_log"), sem("log_a_done")
        suffix_mult, suffix_exp, k_decayed = sem("suffix_mult"), sem("suffix_exp"), sem("k_decayed")
        bias_full = [sem("bias_full0"), sem("bias_full1")]
        fox_turned, fox_qk, fox_masked, fox_scored = (sem(n) for n in ("fox_turned", "fox_qk", "fox_masked", "fox_scored"))
        fox_max, fox_exp, fox_probs, fox_probs_turned = (sem(n) for n in ("fox_max", "fox_exp", "fox_probs", "fox_probs_turned"))
        fox_probs_t, fox_mixed, fox_y_hi, fox_y_lo = (sem(n) for n in ("fox_probs_t", "fox_mixed", "fox_y_hi", "fox_y_lo"))
        gla_q_turned, gla_q_ready, gla_kv, gla_state = (sem(n) for n in ("gla_q_turned", "gla_q_ready", "gla_kv", "gla_state"))
        gla_read, gla_squares, gla_means, gla_rstds = (sem(n) for n in ("gla_read", "gla_squares", "gla_means", "gla_rstds"))
        gla_y, gla_y_turned, gla_y_hi, gla_y_lo = (sem(n) for n in ("gla_y", "gla_y_turned", "gla_y_hi", "gla_y_lo"))
        tail_full = sem("tail_full")
        out_ready, stored = sem("out_ready"), sem("stored")

        def chunk_rows(c):
            return slice((c % 2) * CHUNK, (c % 2) * CHUNK + CHUNK), c // 2

        block = ctx.enter_context(nc.Block())

        @block.sync
        def _(sp):
            def slot_free(blk):
                sp.wait_ge(lo_split, blk - RING + 1)

            def load(blk, src):
                if blk >= RING:
                    slot_free(blk)
                sp.dma_start(raw[:, blk % RING, :, :], src.rearrange("(k p) c -> p k c", p=P))\
                  .then_inc(raw_full[blk % RING], 32)

            def load_pair(slot, j, w_gate, w_up, col):
                half = COLS // 2
                for w, at in ((w_gate, 0), (w_up, half)):
                    sp.dma_start(raw[:, slot, :, at:at + half],
                                 w[0, BK * P * j:BK * P * (j + 1), bass.ds(col, half)]
                                 .rearrange("(k p) c -> p k c", p=P)).then_inc(raw_full[slot], 16)

            def feed_forward(up, down, w_gate, w_up, w_down, kt0, kts):
                b, n = BLOCK[up], PHASES[up][0]
                first = 1 if b == 0 else 0
                if first:
                    for j in range(8):
                        if j >= RING:
                            slot_free(j)
                        load_pair(j % RING, j, w_gate, w_up, 0)
                with sp.Fori(first, n) as i:
                    for j in range(8):
                        slot_free(b + 8 * i + j)
                        load_pair(j % RING, j, w_gate, w_up, kt0 * P + i * (COLS // 2))
                b = BLOCK[down]
                for c in range(4):
                    for j in range(kts // BK):
                        r = (kt0 + BK * j) * P
                        load(b + c * (kts // BK) + j, w_down[0, r:r + BK * P, COLS * c:COLS * (c + 1)])

            def plain(blk, w, row, col):
                load(blk, w[0, row:row + BK * P, col:col + COLS])

            sp.dma_start(gains_rows[0:KD, :], ffn1_norm[0].rearrange("(k p) -> k p", p=P)).then_inc(gains_full, 16)
            sp.dma_start(gains_rows[KD:2 * KD, :], mix_norm[0].rearrange("(k p) -> k p", p=P)).then_inc(gains_full, 16)
            sp.dma_start(gains_rows[2 * KD:3 * KD, :], ffn2_norm[0].rearrange("(k p) -> k p", p=P)).then_inc(gains_full, 16)
            sp.dma_start(gains_rows[3 * KD:4 * KD, :], ple_norm[0].rearrange("(k p) -> k p", p=P)).then_inc(gains_full, 16)
            sp.dma_start(gains_rows[4 * KD:4 * KD + 2, :], gla_head_norm[0].rearrange("(k p) -> k p", p=P)).then_inc(gains_full, 16)
            feed_forward("up1a", "down1a", ffn1_w_gate, ffn1_w_up, ffn1_w_down, 0, HALF_KT[0])
            feed_forward("up1b", "down1b", ffn1_w_gate, ffn1_w_up, ffn1_w_down, HALF_KT[0], HALF_KT[1])
            for g in range(12):
                col = COLS * g + (HEADS if g >= 6 else 0)
                for j in range(8):
                    plain(BLOCK["project"] + 8 * g + j, w_in, BK * P * j, col)
            for g in range(8):
                for j in range(8):
                    plain(BLOCK["merge"] + 8 * g + j, w_merge_gate, BK * P * j, COLS * g)
            for c in range(4):
                for n, w in enumerate((w_branch_fox, w_branch_gla)):
                    for j in range(4):
                        plain(BLOCK["branch"] + 8 * c + 4 * n + j, w, BK * P * j, COLS * c)
            for g in range(4):
                for j in range(8):
                    plain(BLOCK["out"] + 8 * g + j, w_out, BK * P * j, COLS * g)
            feed_forward("up2a", "down2a", ffn2_w_gate, ffn2_w_up, ffn2_w_down, 0, HALF_KT[0])
            feed_forward("up2b", "down2b", ffn2_w_gate, ffn2_w_up, ffn2_w_down, HALF_KT[0], HALF_KT[1])
            for c in range(4):
                for j in range(8):
                    plain(BLOCK["ple"] + 9 * c + j, w_ple_gate, BK * P * j, COLS * c)
                plain(BLOCK["ple"] + 9 * c + 8, w_ple_proj, 0, COLS * c)
            for n in range(4):
                sp.wait_ge(out_ready, n + 1)
                t, at = n // 2, (n % 2) * (D // 2)
                sp.dma_start(out_tm[:, t, at:at + D // 2], h[:, t, at:at + D // 2]).then_inc(stored, 16)
            sp.wait_ge(stored, 64)

        @block.gpsimd
        def _(pool):
            def select(ap, pattern, base, channel, fill, op=ALU.is_ge):
                nc.gpsimd.affine_select(out=ap, in_=ap, pattern=pattern, compare_op=op, fill=fill,
                                        base=base, channel_multiplier=channel).then_inc(pool_chain, 1)

            nc.gpsimd.memset(ident[:], 0.0).then_inc(pool_chain, 1)
            nc.gpsimd.memset(ones[:], 1.0).then_inc(pool_chain, 1)
            nc.gpsimd.memset(up_to[:], 1.0).then_inc(pool_chain, 1)
            nc.gpsimd.memset(later_in_chunk[:], 1.0).then_inc(pool_chain, 1)
            nc.gpsimd.memset(behind[:], 1.0).then_inc(pool_chain, 1)
            nc.gpsimd.memset(causal[:], 0.0).then_inc(pool_chain, 1)
            nc.gpsimd.memset(in_chunk[:], 1.0).then_inc(pool_chain, 1)
            nc.gpsimd.memset(minus_half[:], -0.5).then_inc(pool_chain, 1)
            nc.gpsimd.memset(down_t, 1.0).then_inc(pool_chain, 1)
            pool.wait_ge(pool_chain, 9)
            select(ident[:], [[-1, P]], 0, 1, 1.0, ALU.not_equal)
            pool.wait_ge(pool_chain, 10)
            select(up_to[:], [[1, P]], 0, -1, 0.0)
            select(later_in_chunk[:], [[-1, P]], -1, 1, 0.0)
            select(behind[:], [[P, TT], [-1, TOK]], -1, 1, 0.0)
            select(causal[:, 0:P], [[-1, P]], 0, 1, NEG)
            select(causal[:, 2 * P:3 * P], [[-1, P]], 0, 1, NEG)
            select(in_chunk[:, 0:1], [[0, 1]], CHUNK - 1, -1, 0.0)
            select(in_chunk[:, 1:2], [[0, 1]], -CHUNK, 1, 0.0)
            pool.wait_ge(pool_chain, 17)
            select(later_in_chunk[:, 0:CHUNK], [[0, CHUNK]], CHUNK - 1, -1, 0.0)
            pool.wait_ge(pool_chain, 18)
            nc.gpsimd.memset(meansq[:], 1.0).then_inc(consts, 1)

            pool.dma_start(forget_bias[:], fox_forget_bias[0:1, :].to_broadcast([P, HEADS])).then_inc(thin_full, 16)
            pool.dma_start(thin_raw[:, :, 0:HEADS],
                           w_in[0, :, FLOG:FLOG + HEADS].rearrange("(k p) c -> p k c", p=P)).then_inc(thin_full, 16)
            pool.dma_start(thin_raw[:, :, HEADS:THIN],
                           w_in[0, :, GDOWN:GDOWN + RANK].rearrange("(k p) c -> p k c", p=P)).then_inc(thin_full, 16)
            pool.dma_start(gate_up[0:RANK, :], gla_gate_up[0]).then_inc(thin_full, 16)
            pool.dma_start(gate_up[RANK:RANK + 1, :], gla_gate_bias[0:1, :]).then_inc(thin_full, 16)

            def root(n):
                pool.wait_ge(meansq_done, n + 1)
                nc.gpsimd.tensor_tensor(rstd[:], meansq[:], minus_half[:], ALU.pow).then_inc(rstd_done, 1)

            def load_bias(g):
                if g >= 2:
                    pool.wait_ge(read_out, GROUP["merge"] + g - 1)
                pool.dma_start(merge_bias[:, g % 2, :],
                               b_merge_gate[0:1, COLS * g:COLS * (g + 1)].to_broadcast([P, COLS]))\
                    .then_inc(bias_full[g % 2], 16)

            def mask_log_f(head):
                if head >= 2:
                    pool.wait_ge(fox_scored, head - 1)
                m = masked_log_f[:, head % 2, :, :]
                for n, (mask, t) in enumerate(((up_to, 0), (ones, 0), (up_to, 1))):
                    nc.gpsimd.tensor_scalar(m[:, n, :], mask[:], log_f[:, t, head:head + 1], None, ALU.mult)\
                        .then_inc(fox_masked, 1)

            root(0)
            root(1)
            load_bias(0)
            load_bias(1)
            pool.wait_ge(log_f_done, 1)
            mask_log_f(0)
            mask_log_f(1)
            for g in range(1, 8):
                if g % 2 == 0:
                    pool.wait_ge(gla_means, g // 2)
                    nc.gpsimd.tensor_tensor(gla_rstd[:], gla_meansq[:], minus_half[:], ALU.pow).then_inc(gla_rstds, 1)
                if g + 1 < 8:
                    load_bias(g + 1)
                    mask_log_f(g + 1)
            pool.wait_ge(gla_means, 4)
            nc.gpsimd.tensor_tensor(gla_rstd[:], gla_meansq[:], minus_half[:], ALU.pow).then_inc(gla_rstds, 1)
            root(2)
            root(3)
            pool.wait_ge(multiplied, BLOCK["ple"])
            pool.dma_start(p_tm, p[0, 0].rearrange("(t p) c -> p t c", p=P)).then_inc(tail_full, 16)
            pool.dma_start(final_gain, final_norm.rearrange("(a d) -> a d", a=1).to_broadcast([P, D])).then_inc(tail_full, 16)
            root(4)

        @block.scalar
        def _(act):
            chain = [0]

            def after_own(ins):
                chain[0] += 1
                ins.then_inc(act_chain, 1)
                act.wait_ge(act_chain, chain[0])

            def split(blk, slot, full):
                act.wait_ge(raw_full[slot], 32 * full)
                if not isinstance(blk, int) or blk >= RING:
                    act.wait_ge(multiplied, blk - RING + 1)
                nc.scalar.activation(w_hi[:, slot, :, :], raw[:, slot, :, :], ACT.Copy).then_inc(hi_split, 1)

            def splits(blk, j0, j1, full=None):
                for j in range(j0, j1):
                    if full is None:
                        split(blk + j, (blk + j) % RING, (blk + j) // RING + 1)
                    else:
                        split(blk + j, j % RING, full + j // RING)

            def turn_gained(t, hi, kt, gain):
                act.wait_ge(turned, t + 1)
                for k in range(2):
                    last = nc.scalar.activation(hi[:, kt + k, :], turn_bank[t % 2][:, k * TOK:(k + 1) * TOK],
                                                ACT.Copy, scale=gains[:, gain + kt + k:gain + kt + k + 1])
                last.then_inc(turned_hi, 1)

            def turn_plain(t, bank, out_ap):
                act.wait_ge(turned, t + 1)
                nc.scalar.activation(out_ap, turn_bank[bank][:, :].rearrange("p (k c) -> p k c", k=2), ACT.Copy)\
                    .then_inc(turned_hi, 1)

            def square(c):
                for t in range(TT):
                    last = nc.scalar.activation(scratch[:, t, :], h[:, t, COLS * c:COLS * (c + 1)], ACT.Square,
                                                accum_out=sumsq[:, t, c:c + 1])
                last.then_inc(sumsq_done, 1)

            def silu(g, first_bank, n):
                act.wait_ge(multiplied, g)
                for t in range(TT):
                    last = nc.scalar.activation(scratch[:, t, 0:TOK], acc[first_bank + t][:, 0:TOK], ACT.Silu,
                                                scale=rstd[:, t:t + 1])
                last.then_inc(silu_done, 1)

            def no_tail():
                pass

            def up_phase(name, norm, tail_out, tail_split):
                b, n, t0 = BLOCK[name], PHASES[name][0], TURN[name]
                splits(b, 0, 4)
                tail_out()
                splits(b, 4, 6)
                tail_split()
                splits(b, 6, 8)
                act.wait_ge(rstd_done, norm + 1)
                with act.Fori(0, n // 2 - 1) as i:
                    for s in range(2):
                        start = b + 8 * (s + 1) + 16 * i
                        full = b // RING + 2 * (s + 1) + 4 * i + 1
                        splits(start, 0, 4, full)
                        silu(start, 2 * s, None)
                        splits(start, 4, 6, full)
                        turn_hidden(t0 + s + 2 * i, (t0 + s) % 2, s + 2 * i)
                        splits(start, 6, 8, full)
                start = b + 8 * (n - 1)
                splits(start, 0, 4)
                silu(start, 0, None)
                splits(start, 4, 6)
                turn_hidden(t0 + n - 2, (t0 + n) % 2, n - 2)
                splits(start, 6, 8)

            def turn_hidden(t, bank, group):
                turn_plain(t, bank, slab_r[:, bass.ds(BK * group, BK), :])

            def down_phase(up, down, kts, squares, hi=None, gain=None):
                b, g, n, nb = BLOCK[down], GROUP[down], PHASES[up][0], kts // BK
                for c in range(4):
                    start = b + nb * c
                    splits(start, 0, 4)
                    if c == 0:
                        silu(start, 2, None)
                    splits(start, 4, 6)
                    if c == 0:
                        turn_hidden(TURN[up] + n - 1, (TURN[up] + n - 1) % 2, n - 1)
                    elif squares:
                        turn_rows(down, c - 1, hi, gain)
                    splits(start, 6, nb)

            def turn_rows(name, c, hi, gain):
                act.wait_ge(read_out, GROUP[name] + c + 1)
                square(c)
                for k in range(2):
                    turn_gained(TURN[name] + 2 * c + k, hi, 4 * c + 2 * k, gain)

            for c in range(4):
                act.dma_start(h[:, :, COLS * c:COLS * (c + 1)], x_tm[:, :, COLS * c:COLS * (c + 1)]).then_inc(x_full[c], 16)

            b = BLOCK["up1a"]
            act.wait_ge(gains_ready, 1)
            for j in range(8):
                turn_gained(j, x_hi, 2 * j, 0)
                if j % 2:
                    act.wait_ge(x_full[j // 2], 16)
                    square(j // 2)
                split(b + j, j % RING, j // RING + 1)
            act.wait_ge(rstd_done, 1)
            n, t0 = PHASES["up1a"][0], TURN["up1a"]
            with act.Fori(0, n // 2 - 1) as i:
                for s in range(2):
                    start = b + 8 * (s + 1) + 16 * i
                    full = b // RING + 2 * (s + 1) + 4 * i + 1
                    splits(start, 0, 4, full)
                    silu(start, 2 * s, None)
                    splits(start, 4, 6, full)
                    turn_hidden(t0 + s + 2 * i, (t0 + s) % 2, s + 2 * i)
                    splits(start, 6, 8, full)
            start = b + 8 * (n - 1)
            splits(start, 0, 4)
            silu(start, 0, None)
            splits(start, 4, 6)
            turn_hidden(t0 + n - 2, (t0 + n) % 2, n - 2)
            splits(start, 6, 8)
            down_phase("up1a", "down1a", HALF_KT[0], False)
            up_phase("up1b", 0, no_tail, no_tail)
            down_phase("up1b", "down1b", HALF_KT[1], True, x_hi, KD)

            b, g0 = BLOCK["project"], GROUP["project"]

            def project_out(after, bank, slab0, func=ACT.Copy):
                act.wait_ge(multiplied, after)
                for t in range(TT):
                    last = nc.scalar.activation(slab[:, bass.ds(slab0, 4), t, :],
                                                acc[bank + t][:, :].rearrange("p (s c) -> p s c", s=4),
                                                func, scale=rstd[:, t:t + 1])
                last.then_inc(read_out, 1)

            splits(b, 0, 6)
            turn_rows("down1b", 3, x_hi, KD)
            splits(b, 6, 8)
            act.wait_ge(thin_full, 80)
            nc.scalar.activation(thin_hi, thin_raw, ACT.Copy).then_inc(thin_hi_done, 1)
            act.wait_ge(rstd_done, 2)
            with act.Fori(0, 4) as i:
                for s in range(2):
                    start = b + 8 * (s + 1) + 16 * i
                    full = b // RING + 2 * (s + 1) + 4 * i + 1
                    splits(start, 0, 4, full)
                    project_out(start, 2 * s, 4 * s + 8 * i)
                    splits(start, 4, 8, full)
            start = b + 8 * 9
            splits(start, 0, 4)
            project_out(start, 0, 32)
            splits(start, 4, 8)
            start += 8
            splits(start, 0, 4)
            project_out(start, 2, 36)
            splits(start, 4, 5)
            act.wait_ge(thin_neg, 1)
            after_own(nc.scalar.activation(thin_e[:], thin_e[:], ACT.Exp))
            nc.scalar.activation(thin_e[:], thin_e[:], ACT.Ln, bias=1.0).then_inc(thin_log, 1)
            splits(start, 5, 8)
            start += 8
            splits(start, 0, 2)
            act.wait_ge(decay_mult, 1)
            for t in range(TT):
                last = nc.scalar.activation(log_a[:, t, :], turn_bank[t][:, :], ACT.Abs)
            after_own(last)
            after_own(nc.scalar.activation(log_a, log_a, ACT.Exp, scale=-1.0))
            nc.scalar.activation(log_a, log_a, ACT.Ln, bias=1.0).then_inc(decay_log, 1)
            splits(start, 2, 4)
            project_out(start, 0, 40, ACT.Silu)
            splits(start, 4, 7)
            act.wait_ge(suffix_mult, 1)
            for t in range(TT):
                nc.scalar.activation(scratch[:, t, :], fox_bank[t][:, :], ACT.Exp, scale=1.0 / TAU)
            nc.scalar.activation(decay[:], turn_bank[0][:, 0:4 * GH], ACT.Exp, scale=1.0 / TAU).then_inc(suffix_exp, 1)
            splits(start, 7, 8)

            def fox_qk_copy(head):
                act.wait_ge(fox_turned, head + 1)
                nc.scalar.activation(qk_t[:, 0:TOK], fox_bank[0][:, 0:TOK], ACT.Copy, scale=DH ** -0.5)
                nc.scalar.activation(qk_t[:, TOK:], fox_bank[0][:, TOK:], ACT.Copy).then_inc(fox_qk, 1)

            def fox_exponentials(head):
                act.wait_ge(fox_max, head + 1)
                for n, sl in enumerate((slice(0, P), slice(P, 3 * P))):
                    last = nc.scalar.activation(probs[:, sl], probs[:, sl], ACT.Exp, bias=neg_max[:, n:n + 1],
                                                accum_out=row_sum[:, n:n + 1])
                last.then_inc(fox_exp, 1)

            def fox_probs_copy(head):
                act.wait_ge(fox_probs_turned, head + 1)
                nc.scalar.activation(probs_t[:], fox_bank[0][:, 0:3 * P], ACT.Copy).then_inc(fox_probs_t, 1)

            def fox_result(head):
                act.wait_ge(fox_mixed, head + 1)
                nc.scalar.activation(slab_r[:, FQ + head, :], fox_bank[1][:, 0:TOK], ACT.Copy).then_inc(fox_y_hi, 1)

            def gla_queries(pair):
                act.wait_ge(gla_q_turned, pair + 1)
                nc.scalar.activation(gq_t[:], turn_bank[0][:, :].rearrange("p (h c) -> p h c", h=2), ACT.Copy,
                                     scale=DK ** -0.5).then_inc(gla_q_ready, 1)

            def gla_square(n):
                act.wait_ge(gla_read, 2 * n + 2)
                for hh in range(2):
                    last = nc.scalar.activation(scratch[:, hh, 0:DV], turn_bank[1][:, hh * DV:(hh + 1) * DV],
                                                ACT.Square, accum_out=gla_sumsq[:, hh:hh + 1])
                last.then_inc(gla_squares, 1)

            def gla_result(n):
                act.wait_ge(gla_y_turned, n + 1)
                pair, t = n // 2, n % 2
                turned_y = turn_bank[0][:, :].rearrange("p (h d c) -> p h d c", h=2, d=2)
                for d in range(2):
                    s = GR + 4 * pair + d
                    last = nc.scalar.activation(slab_r[:, s:s + 3:2, t * P:(t + 1) * P], turned_y[:, :, d, :], ACT.Copy,
                                                scale=gains[:, 4 * KD + d:4 * KD + d + 1])
                last.then_inc(gla_y_hi, 1)

            b = BLOCK["merge"]
            for g in range(8):
                start = b + 8 * g
                splits(start, 0, 1)
                if g in (3, 5, 7):
                    gla_result((g - 3) // 2)
                splits(start, 1, 2)
                if g > 0:
                    fox_probs_copy(g - 1)
                    if g % 2 == 0:
                        gla_square(g // 2 - 1)
                splits(start, 2, 4)
                if g == 0:
                    project_out(start, 2, 44, ACT.Silu)
                else:
                    fox_result(g - 1)
                splits(start, 4, 5)
                fox_qk_copy(g)
                if g % 4 == 0:
                    gla_queries(g // 4)
                splits(start, 5, 8)
                fox_exponentials(g)

            def gate_sigmoid(n):
                nc.scalar.activation(gates[:, n, :, :], gates[:, n, :, :], ACT.Sigmoid).then_inc(sigmoid_done, 1)

            def turn_merged(c):
                for k in range(2):
                    t = TURN["branch"] + 2 * c + k
                    turn_plain(t, t % 2, x_hi[:, 4 * c + 2 * k:4 * c + 2 * k + 2, :])

            b = BLOCK["branch"]
            for c in range(4):
                start = b + 8 * c
                splits(start, 0, 2)
                if c == 0:
                    fox_probs_copy(7)
                    gla_square(3)
                splits(start, 2, 4)
                if c == 0:
                    fox_result(7)
                    act.wait_ge(read_out, GROUP["merge"] + 8)
                else:
                    gate_sigmoid(4 + c - 1)
                splits(start, 4, 6)
                if c == 0:
                    gla_result(3)
                splits(start, 6, 7)
                if c > 0:
                    turn_merged(c - 1)
                splits(start, 7, 8)
                gate_sigmoid(c)

            b = BLOCK["out"]
            for c in range(4):
                start = b + 8 * c
                splits(start, 0, 4)
                if c == 0:
                    gate_sigmoid(7)
                splits(start, 4, 6)
                if c > 0:
                    turn_rows("out", c - 1, y_r, 2 * KD)
                splits(start, 6, 7)
                if c == 0:
                    turn_merged(3)
                splits(start, 7, 8)

            up_phase("up2a", 2, no_tail, lambda: turn_rows("out", 3, y_r, 2 * KD))
            down_phase("up2a", "down2a", HALF_KT[0], False)
            up_phase("up2b", 2, no_tail, no_tail)
            down_phase("up2b", "down2b", HALF_KT[1], True, x_hi, 3 * KD)

            def ple_gate(c):
                if c > 0:
                    act.wait_ge(read_out, GROUP["ple"] + 2 * c)
                act.wait_ge(multiplied, BLOCK["ple"] + 9 * c + 8)
                for t in range(TT):
                    last = nc.scalar.activation(scratch[:, t, :], acc[t][:, :], ACT.Sigmoid, scale=rstd[:, t:t + 1])
                last.then_inc(sigmoid_done, 1)

            def square_last(c):
                act.wait_ge(read_out, GROUP["ple"] + 2 * c + 2)
                act.wait_ge(sumsq_done, 16 + c)
                for t in range(TT):
                    last = nc.scalar.activation(turn_bank[t][:, :], h[:, t, COLS * c:COLS * (c + 1)], ACT.Square,
                                                accum_out=sumsq[:, t, c:c + 1])
                last.then_inc(sumsq_done, 1)

            b = BLOCK["ple"]
            for c in range(4):
                start = b + 9 * c
                splits(start, 0, 4)
                if c == 0:
                    splits(start, 4, 6)
                    turn_rows("down2b", 3, x_hi, 3 * KD)
                    splits(start, 6, 8)
                    turn_plain(TURN["p"], TURN["p"] % 2, slab_r[:, P_HI:P_HI + 2, :])
                    act.wait_ge(rstd_done, 4)
                    splits(start, 8, 9)
                else:
                    ple_gate(c - 1)
                    splits(start, 4, 6)
                    square_last(c - 1)
                    splits(start, 6, 9)
            ple_gate(3)
            square_last(3)

        @block.vector
        def _(dve):
            chain = [0]

            def after_own(ins):
                chain[0] += 1
                ins.then_inc(dve_chain, 1)
                dve.wait_ge(dve_chain, chain[0])

            def split(blk, slot):
                dve.wait_ge(hi_split, blk + 1)
                nc.vector.tensor_tensor(w_lo[:, slot, :, :], raw[:, slot, :, :], w_hi[:, slot, :, :].bitcast(F32),
                                        ALU.subtract).then_inc(lo_split, 1)

            def splits(blk, j0, j1, slot0=None):
                for j in range(j0, j1):
                    split(blk + j, (blk + j) % RING if slot0 is None else (slot0 + j) % RING)

            def turn_gained(t, hi, lo, kt, gain):
                dve.wait_ge(turned_hi, t + 1)
                for k in range(2):
                    last = nc.vector.scalar_tensor_tensor(
                        out=lo[:, kt + k, :], in0=turn_bank[t % 2][:, k * TOK:(k + 1) * TOK],
                        scalar=gains[:, gain + kt + k:gain + kt + k + 1], in1=hi[:, kt + k, :].bitcast(F32),
                        op0=ALU.mult, op1=ALU.subtract)
                last.then_inc(turned_lo, 1)

            def turn_plain(t, bank, hi_ap, lo_ap):
                dve.wait_ge(turned_hi, t + 1)
                nc.vector.tensor_tensor(lo_ap, turn_bank[bank][:, :].rearrange("p (k c) -> p k c", k=2),
                                        hi_ap.bitcast(F32), ALU.subtract).then_inc(turned_lo, 1)

            def mean_square(n):
                dve.wait_ge(sumsq_done, 4 * n + 4)
                after_own(nc.vector.tensor_reduce(meansq[:], sumsq[:], AX_X, ALU.add))
                nc.vector.tensor_scalar(meansq[:], meansq[:], 1.0 / D, EPS, ALU.mult, ALU.add).then_inc(meansq_done, 1)

            silus = [0]

            def hidden_out(silu_count, bank):
                dve.wait_ge(silu_done, silu_count)
                for t in range(TT):
                    last = nc.vector.scalar_tensor_tensor(
                        out=scratch[:, t, TOK:], in0=acc[bank + t][:, TOK:], scalar=rstd[:, t:t + 1],
                        in1=scratch[:, t, 0:TOK], op0=ALU.mult, op1=ALU.mult)
                last.then_inc(read_out, 1)

            def turn_hidden(t, bank, group, kts):
                turn_plain(t, bank, slab_r[:, bass.ds(BK * group, BK), :], slab_r[:, bass.ds(kts + BK * group, BK), :])

            def up_groups(name, kts):
                b, n, t0, s0 = BLOCK[name], PHASES[name][0], TURN[name], silus[0]
                with dve.Fori(0, n // 2 - 1) as i:
                    for s in range(2):
                        start = b + 8 * (s + 1) + 16 * i
                        splits(start, 0, 4, 0)
                        hidden_out(s0 + s + 1 + 2 * i, 2 * s)
                        splits(start, 4, 6, 0)
                        turn_hidden(t0 + s + 2 * i, (t0 + s) % 2, s + 2 * i, kts)
                        splits(start, 6, 8, 0)
                start = b + 8 * (n - 1)
                splits(start, 0, 4)
                hidden_out(s0 + n - 1, 0)
                splits(start, 4, 6)
                turn_hidden(t0 + n - 2, (t0 + n) % 2, n - 2, kts)
                splits(start, 6, 8)
                silus[0] += n

            def rows_out(name, c, after, factor):
                dve.wait_ge(multiplied, after)
                for t in range(TT):
                    rows = h[:, t, COLS * c:COLS * (c + 1)]
                    last = nc.vector.scalar_tensor_tensor(out=rows, in0=acc[2 * (c % 2) + t][:, :], scalar=factor,
                                                          in1=rows, op0=ALU.mult, op1=ALU.add)
                last.then_inc(read_out, 1)

            def turn_rows(name, c, hi, lo, gain):
                for k in range(2):
                    turn_gained(TURN[name] + 2 * c + k, hi, lo, 4 * c + 2 * k, gain)

            def down_groups(up, down, kts, hi=None, lo=None, gain=None):
                b, n, nb = BLOCK[down], PHASES[up][0], kts // BK
                for c in range(4):
                    start = b + nb * c
                    splits(start, 0, 4)
                    if c == 0:
                        hidden_out(silus[0], 2)
                    else:
                        rows_out(down, c - 1, start, 0.5)
                    splits(start, 4, 6)
                    if c == 0:
                        turn_hidden(TURN[up] + n - 1, (TURN[up] + n - 1) % 2, n - 1, kts)
                    elif gain is not None:
                        turn_rows(down, c - 1, hi, lo, gain)
                    splits(start, 6, nb)

            def second_part(up, down, before, hi, lo, gain):
                b = BLOCK[up]
                splits(b, 0, 4)
                rows_out(before, 3, b, 0.5)
                splits(b, 4, 8)
                up_groups(up, HALF_KT[1])
                down_groups(up, down, HALF_KT[1], hi, lo, gain)

            dve.wait_ge(gains_turned, 1)
            nc.vector.tensor_copy(gains[:], fox_bank[0][:, 0:4 * KD + 2]).then_inc(gains_ready, 1)
            dve.wait_ge(gains_ready, 1)
            dve.wait_ge(consts, 1)

            b = BLOCK["up1a"]
            for j in range(8):
                turn_gained(j, x_hi, x_lo, 2 * j, 0)
                split(b + j, j % RING)
            mean_square(0)
            dve.wait_ge(rstd_done, 1)
            up_groups("up1a", HALF_KT[0])
            down_groups("up1a", "down1a", HALF_KT[0])
            second_part("up1b", "down1b", "down1a", x_hi, x_lo, KD)

            b = BLOCK["project"]
            splits(b, 0, 4)
            rows_out("down1b", 3, b, 0.5)
            splits(b, 4, 6)
            turn_rows("down1b", 3, x_hi, x_lo, KD)
            mean_square(1)
            splits(b, 6, 8)
            dve.wait_ge(thin_hi_done, 1)
            nc.vector.tensor_tensor(thin_lo, thin_raw, thin_hi.bitcast(F32), ALU.subtract).then_inc(thin_lo_done, 1)
            with dve.Fori(1, 10) as i:
                splits(b + 8 * i, 0, 8, 0)
            start = b + 8 * 10
            splits(start, 0, 5)
            dve.wait_ge(thin_mult, 1)
            dve.wait_ge(rstd_done, 2)
            for t in range(TT):
                last = nc.vector.tensor_scalar(thin_z[:, t, :], fox_bank[0][:, THIN * t:THIN * (t + 1)], rstd[:, t:t + 1],
                                               None, ALU.mult)
            chain[0] += 1
            last.then_inc(dve_chain, 1)
            dve.wait_ge(dve_chain, chain[0])
            for t in range(TT):
                last = nc.vector.tensor_tensor(thin_z[:, t, 0:HEADS], thin_z[:, t, 0:HEADS], forget_bias[:], ALU.add)
            last.then_inc(thin_scaled, 1)
            dve.wait_ge(thin_scaled, 1)
            nc.vector.scalar_tensor_tensor(out=thin_e[:], in0=thin_z[:, :, 0:HEADS], scalar=-1.0,
                                           in1=thin_z[:, :, 0:HEADS], op0=ALU.mult, op1=ALU.min).then_inc(thin_neg, 1)
            splits(start, 5, 7)
            dve.wait_ge(thin_log, 1)
            nc.vector.scalar_tensor_tensor(out=log_f[:], in0=thin_z[:, :, 0:HEADS], scalar=0.0, in1=thin_e[:],
                                           op0=ALU.min, op1=ALU.subtract).then_inc(log_f_done, 1)
            splits(start, 7, 8)
            dve.wait_ge(down_turned, 1)
            nc.vector.tensor_copy(down_t[0:RANK, :], fox_bank[1][0:RANK, 0:TOK]).then_inc(down_ready, 1)
            start += 8
            splits(start, 0, 2)
            dve.wait_ge(decay_log, 1)
            for t in range(TT):
                last = nc.vector.scalar_tensor_tensor(out=log_a[:, t, :], in0=turn_bank[t][:, :], scalar=0.0,
                                                      in1=log_a[:, t, :], op0=ALU.min, op1=ALU.subtract)
            last.then_inc(log_a_done, 1)
            splits(start, 2, 7)
            dve.wait_ge(suffix_exp, 1)
            for t in range(TT):
                keys = slab[:, GK:GK + GH, t, :]
                last = nc.vector.tensor_tensor(keys, keys, scratch[:, t, :].rearrange("p (s c) -> p s c", s=GH), ALU.mult)
            last.then_inc(k_decayed, 1)
            splits(start, 7, 8)

            def merge_out(g, after):
                dve.wait_ge(multiplied, after)
                dve.wait_ge(bias_full[g % 2], 16 * (g // 2 + 1))
                for t in range(TT):
                    last = nc.vector.scalar_tensor_tensor(
                        out=gates[:, g, t, :], in0=acc[2 * (g % 2) + t][:, :], scalar=rstd[:, t:t + 1],
                        in1=merge_bias[:, g % 2, :], op0=ALU.mult, op1=ALU.add)
                last.then_inc(read_out, 1)

            def fox_mask_max(head):
                dve.wait_ge(fox_scored, head + 1)
                after_own(nc.vector.tensor_tensor(probs[:], fox_bank[1][:, 0:3 * P], causal[:], ALU.add))
                nc.vector.tensor_reduce(neg_max[:, 0:1], probs[:, 0:P], AX_X, ALU.max)
                after_own(nc.vector.tensor_reduce(neg_max[:, 1:2], probs[:, P:3 * P], AX_X, ALU.max))
                nc.vector.tensor_scalar(neg_max[:], neg_max[:], -1.0, None, ALU.mult).then_inc(fox_max, 1)

            def fox_normalise(head):
                dve.wait_ge(fox_exp, head + 1)
                after_own(nc.vector.reciprocal(row_inv[:], row_sum[:]))
                nc.vector.tensor_scalar(probs[:, 0:P], probs[:, 0:P], row_inv[:, 0:1], None, ALU.mult)
                nc.vector.tensor_scalar(probs[:, P:3 * P], probs[:, P:3 * P], row_inv[:, 1:2], None, ALU.mult)\
                    .then_inc(fox_probs, 1)

            def fox_result(head):
                dve.wait_ge(fox_y_hi, head + 1)
                nc.vector.tensor_tensor(slab_r[:, FK + head, :], fox_bank[1][:, 0:TOK],
                                        slab_r[:, FQ + head, :].bitcast(F32), ALU.subtract).then_inc(fox_y_lo, 1)

            def gla_update(g):
                pair, c = g // 4, g % 4
                dve.wait_ge(gla_kv, g + 1)
                for hh in range(2):
                    kv = turn_bank[0][:, hh * DV:(hh + 1) * DV]
                    if c == 0:
                        last = nc.vector.tensor_copy(state[:, hh, :], kv)
                    else:
                        at = (2 * pair + hh) * 4 + c
                        last = nc.vector.scalar_tensor_tensor(out=state[:, hh, :], in0=state[:, hh, :],
                                                              scalar=decay[:, at:at + 1], in1=kv,
                                                              op0=ALU.mult, op1=ALU.add)
                last.then_inc(gla_state, 1)

            def gla_mean(n):
                dve.wait_ge(gla_squares, n + 1)
                nc.vector.tensor_scalar(gla_meansq[:], gla_sumsq[:], 1.0 / DV, EPS, ALU.mult, ALU.add).then_inc(gla_means, 1)

            def gla_gate(n):
                pair, t = n // 2, n % 2
                dve.wait_ge(gla_rstds, n + 1)
                for hh in range(2):
                    s = GR + 2 * (2 * pair + hh)
                    last = nc.vector.scalar_tensor_tensor(
                        out=slab[:, s:s + 2, t, :], in0=turn_bank[1][:, hh * DV:(hh + 1) * DV].rearrange("p (d c) -> p d c", d=2),
                        scalar=gla_rstd[:, hh:hh + 1], in1=slab[:, s:s + 2, t, :], op0=ALU.mult, op1=ALU.mult)
                last.then_inc(gla_y, 1)

            def gla_result(n):
                pair, t = n // 2, n % 2
                dve.wait_ge(gla_y_hi, n + 1)
                turned_y = turn_bank[0][:, :].rearrange("p (h d c) -> p h d c", h=2, d=2)
                for d in range(2):
                    at, of = GV + 4 * pair + d, GR + 4 * pair + d
                    last = nc.vector.scalar_tensor_tensor(
                        out=slab_r[:, at:at + 3:2, t * P:(t + 1) * P], in0=turned_y[:, :, d, :],
                        scalar=gains[:, 4 * KD + d:4 * KD + d + 1],
                        in1=slab_r[:, of:of + 3:2, t * P:(t + 1) * P].bitcast(F32), op0=ALU.mult, op1=ALU.subtract)
                last.then_inc(gla_y_lo, 1)

            b = BLOCK["merge"]
            for g in range(8):
                start = b + 8 * g
                splits(start, 0, 1)
                if g in (3, 5, 7):
                    gla_result((g - 3) // 2)
                splits(start, 1, 2)
                if g > 0 and g % 2 == 0:
                    gla_mean(g // 2 - 1)
                splits(start, 2, 3)
                if g > 0 and g % 2 == 0:
                    gla_gate(g // 2 - 1)
                splits(start, 3, 4)
                if g > 0:
                    merge_out(g - 1, start)
                    fox_result(g - 1)
                splits(start, 4, 7)
                gla_update(g)
                fox_mask_max(g)
                splits(start, 7, 8)
                fox_normalise(g)

            def branch_a_out(c, after):
                dve.wait_ge(multiplied, after)
                dve.wait_ge(sigmoid_done, 2 * c + 1)
                for t in range(TT):
                    last = nc.vector.tensor_tensor(gates[:, c, t, :], acc[t][:, :], gates[:, c, t, :], ALU.mult)
                last.then_inc(read_out, 1)

            def branch_b_out(c, after):
                dve.wait_ge(multiplied, after)
                dve.wait_ge(sigmoid_done, 2 * c + 2)
                for t in range(TT):
                    last = nc.vector.tensor_tensor(gates[:, 4 + c, t, :], acc[2 + t][:, :], gates[:, 4 + c, t, :], ALU.mult)
                after_own(last)
                nc.vector.tensor_tensor(gates[:, c, :, :], gates[:, c, :, :], gates[:, 4 + c, :, :], ALU.add).then_inc(read_out, 1)

            def turn_merged(c):
                for k in range(2):
                    t, kt = TURN["branch"] + 2 * c + k, 4 * c + 2 * k
                    turn_plain(t, t % 2, x_hi[:, kt:kt + 2, :], x_lo[:, kt:kt + 2, :])

            b = BLOCK["branch"]
            for c in range(4):
                start = b + 8 * c
                splits(start, 0, 2)
                if c == 0:
                    gla_mean(3)
                splits(start, 2, 3)
                if c == 0:
                    gla_gate(3)
                splits(start, 3, 4)
                if c == 0:
                    merge_out(7, start)
                    fox_result(7)
                else:
                    branch_b_out(c - 1, start)
                splits(start, 4, 6)
                if c == 0:
                    gla_result(3)
                splits(start, 6, 7)
                if c > 0:
                    turn_merged(c - 1)
                splits(start, 7, 8)
                branch_a_out(c, start + 4)

            b = BLOCK["out"]
            for c in range(4):
                start = b + 8 * c
                splits(start, 0, 4)
                if c == 0:
                    branch_b_out(3, start)
                else:
                    rows_out("out", c - 1, start, 1.0)
                splits(start, 4, 6)
                if c > 0:
                    turn_rows("out", c - 1, y_r, y_r[:, KD:, :], 2 * KD)
                splits(start, 6, 7)
                if c == 0:
                    turn_merged(3)
                splits(start, 7, 8)

            b = BLOCK["up2a"]
            splits(b, 0, 4)
            rows_out("out", 3, b, 1.0)
            splits(b, 4, 6)
            turn_rows("out", 3, y_r, y_r[:, KD:, :], 2 * KD)
            mean_square(2)
            splits(b, 6, 8)
            dve.wait_ge(rstd_done, 3)
            up_groups("up2a", HALF_KT[0])
            down_groups("up2a", "down2a", HALF_KT[0])
            second_part("up2b", "down2b", "down2a", x_hi, x_lo, 3 * KD)

            def ple_out(c):
                dve.wait_ge(sigmoid_done, 8 + c + 1)
                dve.wait_ge(multiplied, BLOCK["ple"] + 9 * c + 9)
                for t in range(TT):
                    last = nc.vector.tensor_tensor(scratch[:, t, :], acc[2 + t][:, :], scratch[:, t, :], ALU.mult)
                after_own(last)
                rows = h[:, :, COLS * c:COLS * (c + 1)]
                nc.vector.tensor_tensor(rows, rows, scratch[:, :, :], ALU.add).then_inc(read_out, 2)

            b = BLOCK["ple"]
            for c in range(4):
                start = b + 9 * c
                splits(start, 0, 4)
                if c == 0:
                    rows_out("down2b", 3, b, 0.5)
                    splits(start, 4, 6)
                    turn_rows("down2b", 3, x_hi, x_lo, 3 * KD)
                    mean_square(3)
                    splits(start, 6, 8)
                    turn_plain(TURN["p"], TURN["p"] % 2, slab_r[:, P_HI:P_HI + 2, :], slab_r[:, P_LO:P_LO + 2, :])
                    splits(start, 8, 9)
                else:
                    ple_out(c - 1)
                    splits(start, 4, 9)
            ple_out(3)
            mean_square(4)
            dve.wait_ge(tail_full, 32)
            dve.wait_ge(rstd_done, 5)
            for n in range(4):
                t, at = n // 2, (n % 2) * (D // 2)
                rows = h[:, t, at:at + D // 2]
                nc.vector.scalar_tensor_tensor(out=rows, in0=rows, scalar=rstd[:, t:t + 1], in1=final_gain[:, at:at + D // 2],
                                               op0=ALU.mult, op1=ALU.mult).then_inc(out_ready, 1)

        @block.tensor
        def _(pe):
            def blocks(blk, bank, hi, lo, j0, j1, nb, slot0=None, tiles=None):
                for j in range(j0, j1):
                    slot = (blk + j) % RING if slot0 is None else (slot0 + j) % RING
                    if tiles:
                        tiles(j)
                    pe.wait_ge(lo_split, blk + j + 1)
                    for k in range(BK):
                        kt = BK * j + k
                        for t in range(TT):
                            tok = slice(t * P, (t + 1) * P)
                            to = acc[bank + t][:, :]
                            nc.tensor.matmul(to, hi(kt)[:, tok], w_hi[:, slot, k, :], start=kt == 0, stop=False)
                            nc.tensor.matmul(to, hi(kt)[:, tok], w_lo[:, slot, k, :], start=False, stop=False)
                            last = nc.tensor.matmul(to, lo(kt)[:, tok], w_hi[:, slot, k, :], start=False,
                                                    stop=kt == BK * nb - 1)
                    last.then_inc(multiplied, 1)

            def bank_free(group):
                pe.wait_ge(read_out, group - 1)

            def of(hi_tensor, lo_tensor, hi0=0, lo0=0):
                return (lambda kt: hi_tensor[:, hi0 + kt, :]), (lambda kt: lo_tensor[:, lo0 + kt, :])

            def turn(t, bank, tile):
                if not isinstance(t, int) or t >= 2:
                    pe.wait_ge(turned_lo, t - 1)
                for k in range(2):
                    for tok in range(TT):
                        at = k * TOK + tok * P
                        last = nc.tensor.transpose(turn_bank[bank][:, at:at + P], tile(k, tok), ident[:])
                last.then_inc(turned, 1)

            def turn_rows(name, c):
                pe.wait_ge(read_out, GROUP[name] + c + 1)
                for n in range(2):
                    t = TURN[name] + 2 * c + n
                    turn(t, t % 2, lambda k, tok: h[:, tok, (4 * c + 2 * n + k) * P:(4 * c + 2 * n + k + 1) * P])

            def turn_hidden(t, bank, group):
                pe.wait_ge(read_out, group)
                turn(t, bank, lambda k, tok: scratch[:, tok, TOK + k * P:TOK + (k + 1) * P])

            def tiles_of(first_turn):
                return lambda j: pe.wait_ge(turned_lo, first_turn + j + 1)

            def up_groups(name, hi, lo):
                b, n, t0, g = BLOCK[name], PHASES[name][0], TURN[name], GROUP[name]
                with pe.Fori(0, n // 2 - 1) as i:
                    for s in range(2):
                        start, group = b + 8 * (s + 1) + 16 * i, g + s + 1 + 2 * i
                        bank = 2 * ((s + 1) % 2)
                        bank_free(group)
                        blocks(start, bank, hi, lo, 0, 2, 8, 0)
                        turn_hidden(t0 + s + 2 * i, (t0 + s) % 2, group)
                        blocks(start, bank, hi, lo, 2, 8, 8, 0)
                start, group = b + 8 * (n - 1), g + n - 1
                bank_free(group)
                blocks(start, 2, hi, lo, 0, 2, 8)
                turn_hidden(t0 + n - 2, (t0 + n) % 2, group)
                blocks(start, 2, hi, lo, 2, 8, 8)

            def down_groups(up, down, kts, turns):
                b, g, n, nb = BLOCK[down], GROUP[down], PHASES[up][0], kts // BK
                hi, lo = of(slab_r, slab_r, 0, kts)
                for c in range(4):
                    start, bank = b + nb * c, 2 * (c % 2)
                    bank_free(g + c)
                    tiles = tiles_of(TURN[up]) if c == 0 else None
                    blocks(start, bank, hi, lo, 0, 2, nb, tiles=tiles)
                    if c == 0:
                        turn_hidden(TURN[up] + n - 1, (TURN[up] + n - 1) % 2, g)
                    elif turns:
                        turn_rows(down, c - 1)
                    blocks(start, bank, hi, lo, 2, nb, nb, tiles=tiles)

            pe.wait_ge(consts, 1)
            pe.wait_ge(gains_full, 80)
            nc.tensor.transpose(fox_bank[0][:, 0:4 * KD + 2], gains_rows[:], ident[0:4 * KD + 2, 0:4 * KD + 2])\
                .then_inc(gains_turned, 1)

            def turn_x(n):
                pe.wait_ge(x_full[n // 2], 16)
                turn(n, n % 2, lambda k, tok: h[:, tok, (2 * n + k) * P:(2 * n + k + 1) * P])

            x_of = of(x_hi, x_lo)
            turn_x(0)
            turn_x(1)
            for j in range(8):
                blocks(0, 0, *x_of, j, j + 1, 8, tiles=tiles_of(0))
                if j + 2 < 8:
                    turn_x(j + 2)
            up_groups("up1a", *x_of)
            down_groups("up1a", "down1a", HALF_KT[0], False)
            bank_free(GROUP["up1b"])
            blocks(BLOCK["up1b"], 0, *x_of, 0, 8, 8)
            up_groups("up1b", *x_of)
            down_groups("up1b", "down1b", HALF_KT[1], True)

            b, g0 = BLOCK["project"], GROUP["project"]

            def after_rows(name, phase, hi_lo):
                start = BLOCK[phase]
                tiles = tiles_of(TURN[name])
                bank_free(GROUP[phase])
                blocks(start, 0, *hi_lo, 0, 2, 8, tiles=tiles)
                turn_rows(name, 3)
                blocks(start, 0, *hi_lo, 2, 8, 8, tiles=tiles)

            after_rows("down1b", "project", x_of)
            with pe.Fori(0, 4) as i:
                for s in range(2):
                    bank_free(g0 + s + 1 + 2 * i)
                    blocks(b + 8 * (s + 1) + 16 * i, 2 * ((s + 1) % 2), *x_of, 0, 8, 8, 0)
            bank_free(g0 + 9)
            blocks(b + 8 * 9, 2, *x_of, 0, 8, 8)
            start = b + 8 * 10
            bank_free(g0 + 10)
            blocks(start, 0, *x_of, 0, 1, 8)
            pe.wait_ge(thin_lo_done, 1)
            for t in range(TT):
                for kt in range(KD):
                    to, tok = fox_bank[0][:, THIN * t:THIN * (t + 1)], slice(t * P, (t + 1) * P)
                    nc.tensor.matmul(to, x_hi[:, kt, tok], thin_hi[:, kt, :], start=kt == 0, stop=False)
                    nc.tensor.matmul(to, x_hi[:, kt, tok], thin_lo[:, kt, :], start=False, stop=False)
                    last = nc.tensor.matmul(to, x_lo[:, kt, tok], thin_hi[:, kt, :], start=False, stop=kt == KD - 1)
            last.then_inc(thin_mult, 1)
            blocks(start, 0, *x_of, 1, 4, 8)
            pe.wait_ge(thin_scaled, 1)
            for t in range(TT):
                last = nc.tensor.transpose(fox_bank[1][0:RANK, t * P:(t + 1) * P], thin_z[:, t, HEADS:THIN], ident[:])
            last.then_inc(down_turned, 1)
            blocks(start, 0, *x_of, 4, 6, 8)
            pe.wait_ge(down_ready, 1)
            for t in range(TT):
                last = nc.tensor.matmul(turn_bank[t][:, :], down_t[0:RANK + 1, t * P:(t + 1) * P], gate_up, start=True, stop=True)
            last.then_inc(decay_mult, 1)
            blocks(start, 0, *x_of, 6, 8, 8)
            start += 8
            bank_free(g0 + 11)
            blocks(start, 2, *x_of, 0, 3, 8)
            pe.wait_ge(log_a_done, 1)
            for t in range(TT):
                nc.tensor.matmul(fox_bank[t][:, :], later_in_chunk[:], log_a[:, t, :], start=True, stop=True)
            for hd in range(GH):
                for t in range(TT):
                    at = hd * 4 + 2 * t
                    last = nc.tensor.matmul(turn_bank[0][:, at:at + 2], log_a[:, t, hd * DK:(hd + 1) * DK], in_chunk[:],
                                            start=True, stop=True)
            last.then_inc(suffix_mult, 1)
            blocks(start, 2, *x_of, 3, 8, 8)

            def fox_turn(head):
                if head > 0:
                    pe.wait_ge(fox_probs_t, head)
                else:
                    pe.wait_ge(suffix_exp, 1)
                    pe.wait_ge(read_out, GROUP["project"] + 10)
                for n, s in enumerate((FQ + head, FK + head)):
                    for t in range(TT):
                        at = n * TOK + t * P
                        last = nc.tensor.transpose(fox_bank[0][:, at:at + P], slab[:, s, t, :], ident[:])
                last.then_inc(fox_turned, 1)

            def fox_scores(head):
                pe.wait_ge(fox_qk, head + 1)
                pe.wait_ge(fox_masked, 3 * head + 3)
                if head > 0:
                    pe.wait_ge(fox_y_lo, head)
                m = masked_log_f[:, head % 2, :, :]
                s0, s1 = fox_bank[1][:, 0:P], fox_bank[1][:, P:3 * P]
                nc.tensor.matmul(s0, qk_t[:, 0:P], qk_t[:, TOK:TOK + P], start=True, stop=False)
                nc.tensor.matmul(s0, m[:, 0, :], behind[:, 0, 0:P], start=False, stop=True)
                nc.tensor.matmul(s1, qk_t[:, P:TOK], qk_t[:, TOK:], start=True, stop=False)
                nc.tensor.matmul(s1, m[:, 1, :], behind[:, 0, :], start=False, stop=False)
                nc.tensor.matmul(s1, m[:, 2, :], behind[:, 1, :], start=False, stop=True).then_inc(fox_scored, 1)

            def fox_turn_probs(head):
                pe.wait_ge(fox_probs, head + 1)
                for n in range(3):
                    last = nc.tensor.transpose(fox_bank[0][:, n * P:(n + 1) * P], probs[:, n * P:(n + 1) * P], ident[:])
                last.then_inc(fox_probs_turned, 1)

            def fox_mix(head):
                pe.wait_ge(fox_probs_t, head + 1)
                nc.tensor.matmul(fox_bank[1][:, 0:TOK], slab[:, FV + head, 0, :], probs_t[:, 0:TOK],
                                 start=True, stop=False, skip_group_check=True)
                nc.tensor.matmul(fox_bank[1][:, P:TOK], slab[:, FV + head, 1, :], probs_t[:, TOK:],
                                 start=False, stop=True, skip_group_check=True).then_inc(fox_mixed, 1)

            def gla_turn_queries(pair):
                if pair > 0:
                    pe.wait_ge(gla_state, 4)
                for hh in range(2):
                    for t in range(TT):
                        at = hh * TOK + t * P
                        last = nc.tensor.transpose(turn_bank[0][:, at:at + P], slab[:, GQ + 2 * pair + hh, t, :], ident[:])
                last.then_inc(gla_q_turned, 1)

            def gla_products(g):
                pair, c = g // 4, g % 4
                rows, t = chunk_rows(c)
                pe.wait_ge(gla_q_ready, pair + 1)
                pe.wait_ge(k_decayed, 1)
                if g > 0:
                    pe.wait_ge(gla_state, g)
                if g >= 3:
                    pe.wait_ge(gla_y_lo, (g - 1) // 2)
                for hh in range(2):
                    hd = 2 * pair + hh
                    last = nc.tensor.matmul(turn_bank[0][:, hh * DV:(hh + 1) * DV], slab[rows, GK + hd, t, :],
                                            slab[rows, GV + 2 * hd:GV + 2 * hd + 2, t, :], start=True, stop=True)
                last.then_inc(gla_kv, 1)

            def gla_read_state(g):
                c = g % 4
                rows, t = chunk_rows(c)
                pe.wait_ge(gla_state, g + 1)
                if g >= 2 and c % 2 == 0:
                    pe.wait_ge(gla_y, g // 2)
                for hh in range(2):
                    at = t * P + rows.start
                    last = nc.tensor.matmul(turn_bank[1][rows, hh * DV:(hh + 1) * DV], gq_t[:, hh, at:at + CHUNK],
                                            state[:, hh, :], start=True, stop=True)
                last.then_inc(gla_read, 1)

            def gla_turn_result(n):
                pair, t = n // 2, n % 2
                pe.wait_ge(gla_y, n + 1)
                pe.wait_ge(gla_state, min(2 * n + 3, 8))
                for hh in range(2):
                    for d in range(2):
                        at = (2 * hh + d) * P
                        last = nc.tensor.transpose(turn_bank[0][:, at:at + P], slab[:, GR + 4 * pair + 2 * hh + d, t, :], ident[:])
                last.then_inc(gla_y_turned, 1)

            b, g0 = BLOCK["merge"], GROUP["merge"]
            for g in range(8):
                start, bank = b + 8 * g, 2 * (g % 2)
                bank_free(g0 + g)
                blocks(start, bank, *x_of, 0, 1, 8)
                fox_turn(g)
                if g % 4 == 0:
                    gla_turn_queries(g // 4)
                blocks(start, bank, *x_of, 1, 3, 8)
                fox_scores(g)
                gla_products(g)
                blocks(start, bank, *x_of, 3, 5, 8)
                if g > 0 and g % 2 == 0:
                    gla_turn_result(g // 2 - 1)
                blocks(start, bank, *x_of, 5, 6, 8)
                fox_turn_probs(g)
                gla_read_state(g)
                blocks(start, bank, *x_of, 6, 8, 8)
                fox_mix(g)

            b, g0 = BLOCK["branch"], GROUP["branch"]
            fox_of, gla_of = of(slab_r, slab_r, FQ, FK), of(slab_r, slab_r, GR, GV)

            def turn_merged(c):
                pe.wait_ge(read_out, g0 + 2 * c + 2)
                for n in range(2):
                    t = TURN["branch"] + 2 * c + n
                    turn(t, t % 2, lambda k, tok: gates[:, c, tok, (2 * n + k) * P:(2 * n + k + 1) * P])

            for c in range(4):
                start = b + 8 * c
                bank_free(g0 + 2 * c)
                tiles = (lambda j: pe.wait_ge(fox_y_lo, 2 * j + 2)) if c == 0 else None
                blocks(start, 0, *fox_of, 0, 2, 4, tiles=tiles)
                if c == 0:
                    gla_turn_result(3)
                blocks(start, 0, *fox_of, 2, 3, 4, tiles=tiles)
                if c == 1:
                    pe.wait_ge(gla_y_lo, 4)
                if c > 0:
                    turn_merged(c - 1)
                blocks(start, 0, *fox_of, 3, 4, 4, tiles=tiles)
                bank_free(g0 + 2 * c + 1)
                tiles = (lambda j: pe.wait_ge(gla_y_lo, 2 if j < 2 else 4)) if c == 0 else None
                blocks(start + 4, 2, *gla_of, 0, 4, 4, tiles=tiles)

            b, g0o = BLOCK["out"], GROUP["out"]
            for c in range(4):
                start, bank = b + 8 * c, 2 * (c % 2)
                bank_free(g0o + c)
                tiles = tiles_of(TURN["branch"]) if c == 0 else None
                blocks(start, bank, *x_of, 0, 2, 8, tiles=tiles)
                if c > 0:
                    turn_rows("out", c - 1)
                blocks(start, bank, *x_of, 2, 3, 8, tiles=tiles)
                if c == 0:
                    turn_merged(3)
                blocks(start, bank, *x_of, 3, 8, 8, tiles=tiles)

            y_of = of(y_r, y_r, 0, KD)
            after_rows("out", "up2a", y_of)
            up_groups("up2a", *y_of)
            down_groups("up2a", "down2a", HALF_KT[0], False)
            bank_free(GROUP["up2b"])
            blocks(BLOCK["up2b"], 0, *y_of, 0, 8, 8)
            up_groups("up2b", *y_of)
            down_groups("up2b", "down2b", HALF_KT[1], True)

            b, g0p = BLOCK["ple"], GROUP["ple"]
            p_of = of(slab_r, slab_r, P_HI, P_LO)
            for c in range(4):
                start = b + 9 * c
                pe.wait_ge(read_out, g0p + max(2 * c, 0))
                tiles = tiles_of(TURN["down2b"]) if c == 0 else None
                blocks(start, 0, *x_of, 0, 2, 8, tiles=tiles)
                if c == 0:
                    turn_rows("down2b", 3)
                blocks(start, 0, *x_of, 2, 4, 8, tiles=tiles)
                if c == 0:
                    pe.wait_ge(tail_full, 32)
                    turn(TURN["p"], TURN["p"] % 2, lambda k, tok: p_tm[:, tok, k * P:(k + 1) * P])
                blocks(start, 0, *x_of, 4, 8, 8, tiles=tiles)
                if c == 0:
                    pe.wait_ge(turned_lo, TURN["p"] + 1)
                blocks(start + 8, 2, *p_of, 0, 1, 1)


_INS = ["x", "p", "ffn1_norm", "ffn1_w_gate", "ffn1_w_up", "ffn1_w_down", "mix_norm", "w_in",
        "fox_forget_bias", "gla_gate_up", "gla_gate_bias", "gla_head_norm", "w_branch_fox",
        "w_branch_gla", "w_merge_gate", "b_merge_gate", "w_out", "ffn2_norm", "ffn2_w_gate",
        "ffn2_w_up", "ffn2_w_down", "ple_norm", "w_ple_proj", "w_ple_gate", "final_norm"]


def kernel(**inputs):
    import numpy as np
    import concourse.bacc as bacc
    from concourse.bass_utils import run_bass_kernel_spmd

    nc = bacc.Bacc("TRN2", target_bir_lowering=False, num_devices=1)
    arrays, args = {}, []
    for name in _INS:
        a = np.ascontiguousarray(inputs[name])
        arrays[f"in_{name}"] = a
        args.append(nc.dram_tensor(f"in_{name}", a.shape, mybir.dt.from_np(a.dtype), kind="ExternalInput").ap())
    args.append(nc.dram_tensor("out_0", (1, TOK, D), F32, kind="ExternalOutput").ap())
    build(nc, *args)
    r = run_bass_kernel_spmd(nc, [arrays], core_ids=[0])
    return r.results[0]["out_0"]
```

```python
from contextlib import ExitStack

import concourse.bass as bass
from concourse import mybir

P = 128
F32 = mybir.dt.float32
F32R = mybir.dt.float32r
ALU = mybir.AluOpType
ACT = mybir.ActivationFunctionType
AX_X = mybir.AxisListType.X

TOK = 256
TT = TOK // P
D = 2048
KD = D // P
FF = 5632
HALF_KT = (24, FF // P - 24)
HEADS = 8
DH = 128
GH = 4
DK = 128
DV = 256
RANK = 16
TAU = 16.0
CHUNK = 64
EPS = 1e-6
COLS = 512
BK = 2
RING = 4
NEG = -3.0e38

FQ, FK, FV, GQ, GK, GV, GR = 0, 8, 16, 24, 28, 32, 40
SLABS = 48
FLOG = 3 * HEADS * DH
GLA0 = FLOG + HEADS
GDOWN = GLA0 + 2 * GH * DK + 2 * GH * DV
THIN = HEADS + RANK
THIN_FOX = 32

PHASES = {
    "up1a": (12, 8), "down1a": (4, 12), "up1b": (10, 8), "down1b": (4, 10),
    "project": (12, 8), "merge": (8, 8), "branch": (8, 4), "out": (4, 8),
    "up2a": (12, 8), "down2a": (4, 12), "up2b": (10, 8), "down2b": (4, 10),
    "ple": (4, 9),
}
PLE_GROUPS = (("E", 0, 0, "acc0"), ("E", 1, 1, "fox"), ("G", 0, 2, "acc2"), ("E", 2, 10, "fox"),
              ("G", 1, 11, "acc0"), ("E", 3, 19, "fox"), ("G", 2, 20, "acc2"), ("G", 3, 28, "acc0"))
TURNS = {"x": 8, "up1a": 12, "up1b": 10, "down1b": 8, "branch": 8, "out": 8,
         "up2a": 12, "up2b": 10, "p": 1, "down2b": 8}


def starts():
    block, group, b, g = {}, {}, 0, 0
    for name, (n, nb) in PHASES.items():
        block[name], group[name] = b, g
        b += n * nb
        g += n
    turn, t = {}, 0
    for name, n in TURNS.items():
        turn[name] = t
        t += n
    return block, group, turn, b


def build(nc, x, p, ffn1_norm, ffn1_w_gate, ffn1_w_up, ffn1_w_down, mix_norm, w_in,
          fox_forget_bias, gla_gate_up, gla_gate_bias, gla_head_norm, w_branch_fox, w_branch_gla,
          w_merge_gate, b_merge_gate, w_out, ffn2_norm, ffn2_w_gate, ffn2_w_up, ffn2_w_down,
          ple_norm, w_ple_proj, w_ple_gate, final_norm, out):
    BLOCK, GROUP, TURN, END = starts()
    x_tm = x[0].rearrange("(t p) d -> p t d", p=P)
    out_tm = out[0].rearrange("(t p) d -> p t d", p=P)

    with ExitStack() as ctx:
        def sb(name, shape, dt=F32):
            return ctx.enter_context(nc.sbuf_tensor(name, shape, dt))

        def shared(*views):
            size, made = 0, []
            for name, shape, dt in views:
                with nc.sbuf_tensor(name, shape, dt) as made_one:
                    made.append(made_one)
                n = 4
                for s in shape[1:]:
                    n *= s
                size = max(size, n)
            sb(views[0][0] + "_room", [P, size // 4])
            return made

        def sem(name):
            return ctx.enter_context(nc.semaphore(name))

        h = sb("h", [P, TT, D])
        x_hi, x_lo = sb("x_hi", [P, KD, TOK], F32R), sb("x_lo", [P, KD, TOK], F32R)
        slab_r, slab = shared(("slab_r", [P, SLABS, TOK], F32R), ("slab", [P, SLABS, TT, P], F32))
        gates, y_r = shared(("gates", [P, 8, TT, COLS], F32), ("y_r", [P, 2 * KD, TOK], F32R))
        raw = sb("raw", [P, RING, BK, COLS])
        w_hi, w_lo = sb("w_hi", [P, RING, BK, COLS], F32R), sb("w_lo", [P, RING, BK, COLS], F32R)
        scratch = sb("scratch", [P, TT, COLS])
        ident = sb("ident", [P, P])
        later_in_chunk = sb("later_in_chunk", [P, P])
        up_to = sb("up_to", [P, P])
        ones = sb("ones", [P, P])
        behind = sb("behind", [P, TT, TOK])
        causal = sb("causal", [P, 3 * P])
        in_chunk = sb("in_chunk", [P, 2])
        gains_rows = sb("gains_rows", [4 * KD + 2, P])
        gains = sb("gains", [P, 4 * KD + 2])
        minus_half = sb("minus_half", [P, 2])
        sumsq = sb("sumsq", [P, TT, 4])
        meansq = sb("meansq", [P, TT])
        rstd = sb("rstd", [P, TT])
        merge_bias = sb("merge_bias", [P, 2, COLS])
        forget_bias = sb("forget_bias", [P, HEADS])
        thin_rows = sb("thin_rows", [P, TOK])
        thin_z = sb("thin_z", [P, TT, 2 * THIN_FOX])
        thin_e = sb("thin_e", [P, TT, HEADS])
        log_f = sb("log_f", [P, TT, HEADS])
        qk_t = sb("qk_t", [P, 2 * TOK])
        masked_log_f = sb("masked_log_f", [P, 2, 3, P])
        probs = sb("probs", [P, 3 * P])
        probs_t = sb("probs_t", [P, 3 * P])
        neg_max, row_sum, row_inv = sb("neg_max", [P, 2]), sb("row_sum", [P, 2]), sb("row_inv", [P, 2])
        gq_t = sb("gq_t", [P, 2, TOK])
        state = sb("state", [P, 2, DV])
        decay = sb("decay", [P, GH * 4])
        gla_sumsq, gla_meansq, gla_rstd = sb("gla_sumsq", [P, 2]), sb("gla_meansq", [P, 2]), sb("gla_rstd", [P, 2])
        log_a = gates[:, 7, :, :]
        thin_flat = gates[:, 6, :, :].rearrange("p t c -> p (t c)")
        thin_raw = thin_flat[:, 0:KD * THIN].rearrange("p (k c) -> p k c", k=KD)
        thin_w = y_r[:, 0:8, :].rearrange("p a (b c) -> p (a b) c", c=P)
        gate_up = gates[0:RANK + 1, 5, 0, :]
        down_t = gates[0:32, 5, 1, 0:TOK]
        embedding = gates[:, 0:4, :, :]
        final_gain = gates[:, 4:6, :, :].rearrange("p g t c -> p (g t c)")
        p_tm = gates[:, 6, 0, :].rearrange("p (t c) -> p t c", t=TT)
        P_HI, P_LO = 2 * KD - 4, 2 * KD - 2

        acc = [ctx.enter_context(nc.psum_tensor(f"acc{i}", [P, COLS], F32)) for i in range(4)]
        turn_bank = [ctx.enter_context(nc.psum_tensor(f"turn{i}", [P, COLS], F32)) for i in range(2)]
        fox_bank = [ctx.enter_context(nc.psum_tensor(f"fox{i}", [P, COLS], F32)) for i in range(2)]

        raw_full = [sem(f"raw_full{i}") for i in range(RING)]
        hi_split = sem("hi_split")
        lo_split = sem("lo_split")
        multiplied = sem("multiplied")
        read_out = sem("read_out")
        turned = sem("turned")
        turned_hi = sem("turned_hi")
        turned_lo = sem("turned_lo")
        x_full = [sem(f"x_full{i}") for i in range(KD // BK)]
        first_gains_full, gains_full = sem("first_gains_full"), sem("gains_full")
        gains_turned, gains_ready = sem("gains_turned"), sem("gains_ready")
        ident_ready, consts = sem("ident_ready"), sem("consts")
        pool_chain = sem("pool_chain")
        silu_done = sem("silu_done")
        sumsq_done = sem("sumsq_done")
        meansq_done, rstd_done = sem("meansq_done"), sem("rstd_done")
        sigmoid_done = sem("sigmoid_done")
        dve_chain = sem("dve_chain")
        act_chain = sem("act_chain")
        thin_full, thin_zeroed, thin_hi_done, thin_lo_done = (sem(n) for n in ("thin_full", "thin_zeroed", "thin_hi_done", "thin_lo_done"))
        thin_copied, thin_turned = sem("thin_copied"), sem("thin_turned")
        thin_mult, thin_scaled, thin_neg, thin_log = (sem(n) for n in ("thin_mult", "thin_scaled", "thin_neg", "thin_log"))
        log_f_done, down_turned, down_ready = sem("log_f_done"), sem("down_turned"), sem("down_ready")
        decay_mult, decay_log, log_a_done = sem("decay_mult"), sem("decay_log"), sem("log_a_done")
        suffix_mult, suffix_exp, k_decayed = sem("suffix_mult"), sem("suffix_exp"), sem("k_decayed")
        bias_full = [sem("bias_full0"), sem("bias_full1")]
        fox_turned, fox_qk, fox_masked, fox_scored = (sem(n) for n in ("fox_turned", "fox_qk", "fox_masked", "fox_scored"))
        fox_max, fox_exp, fox_probs, fox_probs_turned = (sem(n) for n in ("fox_max", "fox_exp", "fox_probs", "fox_probs_turned"))
        fox_probs_t, fox_mixed, fox_y_hi, fox_y_lo = (sem(n) for n in ("fox_probs_t", "fox_mixed", "fox_y_hi", "fox_y_lo"))
        gla_q_turned, gla_q_ready, gla_kv, gla_state = (sem(n) for n in ("gla_q_turned", "gla_q_ready", "gla_kv", "gla_state"))
        gla_read, gla_squares, gla_means, gla_rstds = (sem(n) for n in ("gla_read", "gla_squares", "gla_means", "gla_rstds"))
        gla_y, gla_y_turned, gla_y_hi, gla_y_lo = (sem(n) for n in ("gla_y", "gla_y_turned", "gla_y_hi", "gla_y_lo"))
        tail_full = sem("tail_full")
        embedded = sem("embedded")
        gained = sem("gained")
        last_gate = sem("last_gate")
        final_rows, final_squares = sem("final_rows"), sem("final_squares")
        final_means, final_rstds = sem("final_means"), sem("final_rstds")
        out_ready_act, out_ready_dve, stored = sem("out_ready_act"), sem("out_ready_dve"), sem("stored")

        ple_banks = {"acc0": acc[0:2], "acc2": acc[2:4], "fox": fox_bank}

        def chunk_rows(c):
            return slice((c % 2) * CHUNK, (c % 2) * CHUNK + CHUNK), c // 2

        block = ctx.enter_context(nc.Block())

        @block.sync
        def _(sp):
            def slot_free(blk):
                sp.wait_ge(lo_split, blk - RING + 1)

            def load(blk, src):
                if blk >= RING:
                    slot_free(blk)
                sp.dma_start(raw[:, blk % RING, :, :], src.rearrange("(k p) c -> p k c", p=P))\
                  .then_inc(raw_full[blk % RING], 32)

            def load_pair(slot, j, w_gate, w_up, col):
                half = COLS // 2
                for w, at in ((w_gate, 0), (w_up, half)):
                    sp.dma_start(raw[:, slot, :, at:at + half],
                                 w[0, BK * P * j:BK * P * (j + 1), bass.ds(col, half)]
                                 .rearrange("(k p) c -> p k c", p=P)).then_inc(raw_full[slot], 16)

            def feed_forward(up, down, w_gate, w_up, w_down, kt0, kts):
                b, n = BLOCK[up], PHASES[up][0]
                first = 1 if b == 0 else 0
                if first:
                    for j in range(8):
                        piece = slice(BK * P * j, BK * P * (j + 1))
                        sp.dma_start(h[:, :, piece], x_tm[:, :, piece]).then_inc(x_full[j], 16)
                        if j >= RING:
                            slot_free(j)
                        load_pair(j % RING, j, w_gate, w_up, 0)
                with sp.Fori(first, n) as i:
                    for j in range(8):
                        slot_free(b + 8 * i + j)
                        load_pair(j % RING, j, w_gate, w_up, kt0 * P + i * (COLS // 2))
                b = BLOCK[down]
                for c in range(4):
                    for j in range(kts // BK):
                        r = (kt0 + BK * j) * P
                        load(b + c * (kts // BK) + j, w_down[0, r:r + BK * P, COLS * c:COLS * (c + 1)])

            def plain(blk, w, row, col):
                load(blk, w[0, row:row + BK * P, col:col + COLS])

            feed_forward("up1a", "down1a", ffn1_w_gate, ffn1_w_up, ffn1_w_down, 0, HALF_KT[0])
            feed_forward("up1b", "down1b", ffn1_w_gate, ffn1_w_up, ffn1_w_down, HALF_KT[0], HALF_KT[1])
            for g in range(12):
                col = COLS * g + (HEADS if g >= 6 else 0)
                for j in range(8):
                    plain(BLOCK["project"] + 8 * g + j, w_in, BK * P * j, col)
            for g in range(8):
                for j in range(8):
                    plain(BLOCK["merge"] + 8 * g + j, w_merge_gate, BK * P * j, COLS * g)
            for c in range(4):
                for n, w in enumerate((w_branch_fox, w_branch_gla)):
                    for j in range(4):
                        plain(BLOCK["branch"] + 8 * c + 4 * n + j, w, BK * P * j, COLS * c)
            for g in range(4):
                for j in range(8):
                    plain(BLOCK["out"] + 8 * g + j, w_out, BK * P * j, COLS * g)
            feed_forward("up2a", "down2a", ffn2_w_gate, ffn2_w_up, ffn2_w_down, 0, HALF_KT[0])
            feed_forward("up2b", "down2b", ffn2_w_gate, ffn2_w_up, ffn2_w_down, HALF_KT[0], HALF_KT[1])
            for kind, c, first, _ in PLE_GROUPS:
                if kind == "E":
                    plain(BLOCK["ple"] + first, w_ple_proj, 0, COLS * c)
                else:
                    for j in range(8):
                        plain(BLOCK["ple"] + first + j, w_ple_gate, BK * P * j, COLS * c)
            for t in range(TT):
                for n in range(2):
                    for ready, c in ((out_ready_act, n), (out_ready_dve, 2 + n)):
                        sp.wait_ge(ready, 2 * t + n + 1)
                        columns = slice(COLS * c, COLS * (c + 1))
                        sp.dma_start(out_tm[:, t, columns], h[:, t, columns]).then_inc(stored, 16)
            sp.wait_ge(stored, 16 * 4 * TT)

        @block.gpsimd
        def _(pool):
            def select(ap, pattern, base, channel, fill, op=ALU.is_ge):
                nc.gpsimd.affine_select(out=ap, in_=ap, pattern=pattern, compare_op=op, fill=fill,
                                        base=base, channel_multiplier=channel).then_inc(pool_chain, 1)

            nc.gpsimd.memset(ident[:], 0.0).then_inc(pool_chain, 1)
            pool.wait_ge(pool_chain, 1)
            select(ident[:], [[-1, P]], 0, 1, 1.0, ALU.not_equal)
            pool.wait_ge(pool_chain, 2)
            nc.gpsimd.memset(meansq[:], 1.0).then_inc(ident_ready, 1)
            pool.dma_start(gains_rows[KD:2 * KD, :], mix_norm[0].rearrange("(k p) -> k p", p=P)).then_inc(gains_full, 16)
            pool.dma_start(gains_rows[2 * KD:3 * KD, :], ffn2_norm[0].rearrange("(k p) -> k p", p=P)).then_inc(gains_full, 16)
            pool.dma_start(gains_rows[3 * KD:4 * KD, :], ple_norm[0].rearrange("(k p) -> k p", p=P)).then_inc(gains_full, 16)
            pool.dma_start(gains_rows[4 * KD:4 * KD + 2, :], gla_head_norm[0].rearrange("(k p) -> k p", p=P)).then_inc(gains_full, 16)
            nc.gpsimd.memset(ones[:], 1.0).then_inc(pool_chain, 1)
            nc.gpsimd.memset(up_to[:], 1.0).then_inc(pool_chain, 1)
            nc.gpsimd.memset(later_in_chunk[:], 1.0).then_inc(pool_chain, 1)
            nc.gpsimd.memset(behind[:], 1.0).then_inc(pool_chain, 1)
            nc.gpsimd.memset(causal[:], 0.0).then_inc(pool_chain, 1)
            nc.gpsimd.memset(in_chunk[:], 1.0).then_inc(pool_chain, 1)
            nc.gpsimd.memset(down_t, 1.0).then_inc(pool_chain, 1)
            pool.wait_ge(pool_chain, 9)
            select(up_to[:], [[1, P]], 0, -1, 0.0)
            select(later_in_chunk[:], [[-1, P]], -1, 1, 0.0)
            select(behind[:], [[P, TT], [-1, TOK]], -1, 1, 0.0)
            select(causal[:, 0:P], [[-1, P]], 0, 1, NEG)
            select(causal[:, 2 * P:3 * P], [[-1, P]], 0, 1, NEG)
            select(in_chunk[:, 0:1], [[0, 1]], CHUNK - 1, -1, 0.0)
            select(in_chunk[:, 1:2], [[0, 1]], -CHUNK, 1, 0.0)
            pool.wait_ge(pool_chain, 16)
            nc.gpsimd.affine_select(out=later_in_chunk[:, 0:CHUNK], in_=later_in_chunk[:, 0:CHUNK], pattern=[[0, CHUNK]],
                                    compare_op=ALU.is_ge, fill=0.0, base=CHUNK - 1, channel_multiplier=-1).then_inc(consts, 1)
            nc.gpsimd.memset(y_r[:, 0:8, :].bitcast(F32), 0.0).then_inc(thin_zeroed, 1)

            pool.dma_start(forget_bias[:], fox_forget_bias[0:1, :].to_broadcast([P, HEADS])).then_inc(thin_full, 16)
            pool.dma_start(thin_raw[:, :, 0:HEADS],
                           w_in[0, :, FLOG:FLOG + HEADS].rearrange("(k p) c -> p k c", p=P)).then_inc(thin_full, 16)
            pool.dma_start(thin_raw[:, :, HEADS:THIN],
                           w_in[0, :, GDOWN:GDOWN + RANK].rearrange("(k p) c -> p k c", p=P)).then_inc(thin_full, 16)
            pool.dma_start(gate_up[0:RANK, :], gla_gate_up[0]).then_inc(thin_full, 16)
            pool.dma_start(gate_up[RANK:RANK + 1, :], gla_gate_bias[0:1, :]).then_inc(thin_full, 16)

            def root(n):
                pool.wait_ge(meansq_done, n + 1)
                nc.gpsimd.tensor_tensor(rstd[:], meansq[:], minus_half[:], ALU.pow).then_inc(rstd_done, 1)

            def load_bias(g):
                if g >= 2:
                    pool.wait_ge(read_out, GROUP["merge"] + g - 1)
                pool.dma_start(merge_bias[:, g % 2, :],
                               b_merge_gate[0:1, COLS * g:COLS * (g + 1)].to_broadcast([P, COLS]))\
                    .then_inc(bias_full[g % 2], 16)

            def mask_log_f(head):
                if head >= 2:
                    pool.wait_ge(fox_scored, head - 1)
                m = masked_log_f[:, head % 2, :, :]
                for n, (mask, t) in enumerate(((up_to, 0), (ones, 0), (up_to, 1))):
                    nc.gpsimd.tensor_scalar(m[:, n, :], mask[:], log_f[:, t, head:head + 1], None, ALU.mult)\
                        .then_inc(fox_masked, 1)

            root(0)
            root(1)
            load_bias(0)
            load_bias(1)
            pool.wait_ge(log_f_done, 1)
            mask_log_f(0)
            mask_log_f(1)
            for g in range(1, 8):
                if g % 2 == 0:
                    pool.wait_ge(gla_means, g // 2)
                    nc.gpsimd.tensor_tensor(gla_rstd[:], gla_meansq[:], minus_half[:], ALU.pow).then_inc(gla_rstds, 1)
                if g + 1 < 8:
                    load_bias(g + 1)
                    mask_log_f(g + 1)
            pool.wait_ge(gla_means, 4)
            nc.gpsimd.tensor_tensor(gla_rstd[:], gla_meansq[:], minus_half[:], ALU.pow).then_inc(gla_rstds, 1)
            root(2)
            pool.wait_ge(multiplied, BLOCK["down2b"])
            pool.dma_start(p_tm, p[0, 0].rearrange("(t p) c -> p t c", p=P)).then_inc(tail_full, 16)
            pool.dma_start(final_gain, final_norm.rearrange("(a d) -> a d", a=1).to_broadcast([P, D])).then_inc(tail_full, 16)
            root(3)
            for t in range(TT):
                pool.wait_ge(final_means, t + 1)
                nc.gpsimd.tensor_tensor(rstd[:, t:t + 1], meansq[:, t:t + 1], minus_half[:, t:t + 1], ALU.pow)\
                    .then_inc(final_rstds, 1)

        @block.scalar
        def _(act):
            chain = [0]

            def after_own(ins):
                chain[0] += 1
                ins.then_inc(act_chain, 1)
                act.wait_ge(act_chain, chain[0])

            def split(blk, slot, full):
                act.wait_ge(raw_full[slot], 32 * full)
                if not isinstance(blk, int) or blk >= RING:
                    act.wait_ge(multiplied, blk - RING + 1)
                nc.scalar.activation(w_hi[:, slot, :, :], raw[:, slot, :, :], ACT.Copy).then_inc(hi_split, 1)

            def splits(blk, j0, j1, full=None):
                for j in range(j0, j1):
                    if full is None:
                        split(blk + j, (blk + j) % RING, (blk + j) // RING + 1)
                    else:
                        split(blk + j, j % RING, full + j // RING)

            def turn_gained(t, hi, kt, gain):
                act.wait_ge(turned, t + 1)
                for k in range(2):
                    last = nc.scalar.activation(hi[:, kt + k, :], turn_bank[t % 2][:, k * TOK:(k + 1) * TOK],
                                                ACT.Copy, scale=gains[:, gain + kt + k:gain + kt + k + 1])
                last.then_inc(turned_hi, 1)

            def turn_plain(t, bank, out_ap):
                act.wait_ge(turned, t + 1)
                nc.scalar.activation(out_ap, turn_bank[bank][:, :].rearrange("p (k c) -> p k c", k=2), ACT.Copy)\
                    .then_inc(turned_hi, 1)

            def square_tile(c, t):
                made = nc.scalar.activation(scratch[:, t, :], h[:, t, COLS * c:COLS * (c + 1)], ACT.Square,
                                            accum_out=sumsq[:, t, c:c + 1])
                if t == TT - 1:
                    made.then_inc(sumsq_done, 1)

            def square(c):
                for t in range(TT):
                    square_tile(c, t)

            def silu(after, first_bank):
                act.wait_ge(multiplied, after)
                for t in range(TT):
                    last = nc.scalar.activation(scratch[:, t, 0:TOK], acc[first_bank + t][:, 0:TOK], ACT.Silu,
                                                scale=rstd[:, t:t + 1])
                last.then_inc(silu_done, 1)

            def no_tail():
                pass

            def up_phase(name, norm, tail_split=no_tail):
                b = BLOCK[name]
                splits(b, 0, 6)
                tail_split()
                splits(b, 6, 8)
                up_groups(name, norm)

            def up_groups(name, norm):
                b, n, t0 = BLOCK[name], PHASES[name][0], TURN[name]
                with act.Fori(0, n // 2 - 1) as i:
                    for s in range(2):
                        start = b + 8 * (s + 1) + 16 * i
                        full = b // RING + 2 * (s + 1) + 4 * i + 1
                        splits(start, 0, 4, full)
                        act.wait_ge(rstd_done, norm + 1)
                        silu(start, 2 * s)
                        splits(start, 4, 6, full)
                        turn_hidden(t0 + s + 2 * i, (t0 + s) % 2, s + 2 * i)
                        splits(start, 6, 8, full)
                start = b + 8 * (n - 1)
                splits(start, 0, 4)
                silu(start, 0)
                splits(start, 4, 6)
                turn_hidden(t0 + n - 2, (t0 + n) % 2, n - 2)
                splits(start, 6, 8)

            def turn_hidden(t, bank, group):
                turn_plain(t, bank, slab_r[:, bass.ds(BK * group, BK), :])

            def down_phase(up, down, kts, squares, hi=None, gain=None, turn_p=False):
                b, g, n, nb = BLOCK[down], GROUP[down], PHASES[up][0], kts // BK
                for c in range(4):
                    start = b + nb * c
                    splits(start, 0, 4)
                    if c == 0:
                        silu(start, 2)
                    splits(start, 4, 6)
                    if c == 0:
                        turn_hidden(TURN[up] + n - 1, (TURN[up] + n - 1) % 2, n - 1)
                    elif squares:
                        turn_rows(down, c - 1, hi, gain)
                    splits(start, 6, nb)
                    if c == 0 and turn_p:
                        turn_plain(TURN["p"], TURN["p"] % 2, y_r[:, P_HI:P_HI + 2, :])

            def turn_rows(name, c, hi, gain):
                act.wait_ge(read_out, GROUP[name] + c + 1)
                square(c)
                for k in range(2):
                    turn_gained(TURN[name] + 2 * c + k, hi, 4 * c + 2 * k, gain)

            act.dma_start(gains_rows[0:KD, :], ffn1_norm[0].rearrange("(k p) -> k p", p=P)).then_inc(first_gains_full, 16)
            act.wait_ge(ident_ready, 1)
            nc.scalar.activation(minus_half[:], meansq[:], ACT.Copy, scale=-0.5)

            b = BLOCK["up1a"]
            act.wait_ge(gains_ready, 1)
            turn_gained(0, x_hi, 0, 0)
            split(b, 0, 1)
            for j in range(1, 8):
                split(b + j, j % RING, j // RING + 1)
                turn_gained(j, x_hi, 2 * j, 0)
                for c, t in {2: [(0, 0)], 3: [(0, 1)], 4: [(1, 0)], 5: [(1, 1)], 6: [(2, 0), (2, 1)],
                             7: [(3, 0), (3, 1)]}.get(j, []):
                    if t == 0:
                        act.wait_ge(x_full[2 * c], 16)
                        act.wait_ge(x_full[2 * c + 1], 16)
                        if c > 0:
                            act.wait_ge(sumsq_done, c)
                    square_tile(c, t)
            up_groups("up1a", 0)
            down_phase("up1a", "down1a", HALF_KT[0], False)
            up_phase("up1b", 0)
            down_phase("up1b", "down1b", HALF_KT[1], True, x_hi, KD)

            b, g0 = BLOCK["project"], GROUP["project"]

            def project_out(after, bank, slab0, func=ACT.Copy):
                act.wait_ge(multiplied, after)
                for t in range(TT):
                    last = nc.scalar.activation(slab[:, bass.ds(slab0, 4), t, :],
                                                acc[bank + t][:, :].rearrange("p (s c) -> p s c", s=4),
                                                func, scale=rstd[:, t:t + 1])
                last.then_inc(read_out, 1)

            splits(b, 0, 6)
            turn_rows("down1b", 3, x_hi, KD)
            splits(b, 6, 8)
            act.wait_ge(thin_full, 80)
            act.wait_ge(thin_zeroed, 1)
            nc.scalar.activation(thin_w[:, :, 0:RANK], thin_raw[:, :, HEADS:THIN], ACT.Copy)
            nc.scalar.activation(thin_w[:, :, THIN_FOX:THIN_FOX + HEADS], thin_raw[:, :, 0:HEADS], ACT.Copy).then_inc(thin_hi_done, 1)
            act.wait_ge(rstd_done, 2)
            with act.Fori(0, 4) as i:
                for s in range(2):
                    start = b + 8 * (s + 1) + 16 * i
                    full = b // RING + 2 * (s + 1) + 4 * i + 1
                    splits(start, 0, 4, full)
                    project_out(start, 2 * s, 4 * s + 8 * i)
                    splits(start, 4, 8, full)
            start = b + 8 * 9
            splits(start, 0, 4)
            project_out(start, 0, 32)
            splits(start, 4, 6)
            act.wait_ge(thin_mult, 1)
            nc.scalar.activation(thin_rows[:], fox_bank[0][:, 0:TOK], ACT.Copy).then_inc(thin_copied, 1)
            splits(start, 6, 8)
            start += 8
            splits(start, 0, 1)
            act.wait_ge(thin_neg, 1)
            after_own(nc.scalar.activation(thin_e[:], thin_e[:], ACT.Exp))
            nc.scalar.activation(thin_e[:], thin_e[:], ACT.Ln, bias=1.0).then_inc(thin_log, 1)
            splits(start, 1, 4)
            project_out(start, 2, 36)
            splits(start, 4, 8)
            act.wait_ge(decay_mult, 1)
            for t in range(TT):
                last = nc.scalar.activation(log_a[:, t, :], turn_bank[t][:, :], ACT.Abs)
            after_own(last)
            after_own(nc.scalar.activation(log_a, log_a, ACT.Exp, scale=-1.0))
            nc.scalar.activation(log_a, log_a, ACT.Ln, bias=1.0).then_inc(decay_log, 1)
            start += 8
            splits(start, 0, 4)
            project_out(start, 0, 40, ACT.Silu)
            splits(start, 4, 7)
            act.wait_ge(suffix_mult, 1)
            for t in range(TT):
                nc.scalar.activation(scratch[:, t, :], fox_bank[t][:, :], ACT.Exp, scale=1.0 / TAU)
            nc.scalar.activation(decay[:], turn_bank[0][:, 0:4 * GH], ACT.Exp, scale=1.0 / TAU).then_inc(suffix_exp, 1)
            splits(start, 7, 8)

            def fox_qk_copy(head):
                act.wait_ge(fox_turned, head + 1)
                nc.scalar.activation(qk_t[:, 0:TOK], fox_bank[0][:, 0:TOK], ACT.Copy, scale=DH ** -0.5)
                nc.scalar.activation(qk_t[:, TOK:], fox_bank[0][:, TOK:], ACT.Copy).then_inc(fox_qk, 1)

            def fox_exponentials(head):
                act.wait_ge(fox_max, head + 1)
                for n, sl in enumerate((slice(0, P), slice(P, 3 * P))):
                    last = nc.scalar.activation(probs[:, sl], probs[:, sl], ACT.Exp, bias=neg_max[:, n:n + 1],
                                                accum_out=row_sum[:, n:n + 1])
                last.then_inc(fox_exp, 1)

            def fox_probs_copy(head):
                act.wait_ge(fox_probs_turned, head + 1)
                nc.scalar.activation(probs_t[:], fox_bank[0][:, 0:3 * P], ACT.Copy).then_inc(fox_probs_t, 1)

            def fox_result(head):
                act.wait_ge(fox_mixed, head + 1)
                nc.scalar.activation(slab_r[:, FQ + head, :], fox_bank[1][:, 0:TOK], ACT.Copy).then_inc(fox_y_hi, 1)

            def gla_queries(pair):
                act.wait_ge(gla_q_turned, pair + 1)
                nc.scalar.activation(gq_t[:], turn_bank[0][:, :].rearrange("p (h c) -> p h c", h=2), ACT.Copy,
                                     scale=DK ** -0.5).then_inc(gla_q_ready, 1)

            def gla_square(n):
                act.wait_ge(gla_read, 2 * n + 2)
                for hh in range(2):
                    last = nc.scalar.activation(scratch[:, hh, 0:DV], turn_bank[1][:, hh * DV:(hh + 1) * DV],
                                                ACT.Square, accum_out=gla_sumsq[:, hh:hh + 1])
                last.then_inc(gla_squares, 1)

            def gla_result(n):
                act.wait_ge(gla_y_turned, n + 1)
                pair, t = n // 2, n % 2
                turned_y = turn_bank[0][:, :].rearrange("p (h d c) -> p h d c", h=2, d=2)
                for d in range(2):
                    s = GR + 4 * pair + d
                    last = nc.scalar.activation(slab_r[:, s:s + 3:2, t * P:(t + 1) * P], turned_y[:, :, d, :], ACT.Copy,
                                                scale=gains[:, 4 * KD + d:4 * KD + d + 1])
                last.then_inc(gla_y_hi, 1)

            b = BLOCK["merge"]
            for g in range(8):
                start = b + 8 * g
                splits(start, 0, 1)
                if g in (3, 5, 7):
                    gla_result((g - 3) // 2)
                splits(start, 1, 2)
                if g > 0:
                    fox_probs_copy(g - 1)
                    if g % 2 == 0:
                        gla_square(g // 2 - 1)
                splits(start, 2, 4)
                if g == 0:
                    project_out(start, 2, 44, ACT.Silu)
                else:
                    fox_result(g - 1)
                splits(start, 4, 5)
                fox_qk_copy(g)
                if g % 4 == 0:
                    gla_queries(g // 4)
                splits(start, 5, 8)
                fox_exponentials(g)

            def gate_sigmoid(n):
                nc.scalar.activation(gates[:, n, :, :], gates[:, n, :, :], ACT.Sigmoid).then_inc(sigmoid_done, 1)

            def turn_merged(c):
                for k in range(2):
                    t = TURN["branch"] + 2 * c + k
                    turn_plain(t, t % 2, x_hi[:, 4 * c + 2 * k:4 * c + 2 * k + 2, :])

            b = BLOCK["branch"]
            for c in range(4):
                start = b + 8 * c
                splits(start, 0, 2)
                if c == 0:
                    fox_probs_copy(7)
                    gla_square(3)
                splits(start, 2, 4)
                if c == 0:
                    fox_result(7)
                    act.wait_ge(read_out, GROUP["merge"] + 8)
                else:
                    gate_sigmoid(4 + c - 1)
                splits(start, 4, 6)
                if c == 0:
                    gla_result(3)
                splits(start, 6, 7)
                if c > 0:
                    turn_merged(c - 1)
                splits(start, 7, 8)
                gate_sigmoid(c)

            b = BLOCK["out"]
            for c in range(4):
                start = b + 8 * c
                splits(start, 0, 4)
                if c == 0:
                    gate_sigmoid(7)
                splits(start, 4, 6)
                if c > 0:
                    turn_rows("out", c - 1, y_r, 2 * KD)
                splits(start, 6, 7)
                if c == 0:
                    turn_merged(3)
                splits(start, 7, 8)

            up_phase("up2a", 2, lambda: turn_rows("out", 3, y_r, 2 * KD))
            down_phase("up2a", "down2a", HALF_KT[0], False)
            up_phase("up2b", 2)
            down_phase("up2b", "down2b", HALF_KT[1], True, x_hi, 3 * KD, True)

            def ple_gate(c):
                _, _, first, banks = next(x for x in PLE_GROUPS if x[:2] == ("G", c))
                if c > 0:
                    act.wait_ge(gained, TT * c)
                act.wait_ge(multiplied, BLOCK["ple"] + first + 8)
                for t in range(TT):
                    nc.scalar.activation(scratch[:, t, :], ple_banks[banks][t][:, :], ACT.Sigmoid,
                                         scale=rstd[:, t:t + 1]).then_inc(sigmoid_done, 1)

            def ple_embedding(c):
                _, _, first, banks = next(x for x in PLE_GROUPS if x[:2] == ("E", c))
                act.wait_ge(multiplied, BLOCK["ple"] + first + 1)
                for t in range(TT):
                    last = nc.scalar.activation(embedding[:, c, t, :], ple_banks[banks][t][:, :], ACT.Copy)
                last.then_inc(embedded, 1)

            def square_last(c):
                act.wait_ge(sumsq_done, 16 + c)
                for t in range(TT):
                    act.wait_ge(gained, 2 * c + t + 1)
                    last = nc.scalar.activation(turn_bank[t][:, :], h[:, t, COLS * c:COLS * (c + 1)], ACT.Square,
                                                accum_out=sumsq[:, t, c:c + 1])
                last.then_inc(sumsq_done, 1)

            b = BLOCK["ple"]
            splits(b, 0, 5)
            ple_embedding(0)
            splits(b, 5, 6)
            ple_embedding(1)
            turn_rows("down2b", 3, x_hi, 3 * KD)
            splits(b, 6, 13)
            act.wait_ge(rstd_done, 4)
            ple_gate(0)
            splits(b, 13, 14)
            ple_embedding(2)
            splits(b, 14, 16)
            square_last(0)
            splits(b, 16, 22)
            ple_gate(1)
            splits(b, 22, 23)
            ple_embedding(3)
            splits(b, 23, 25)
            square_last(1)
            splits(b, 25, 31)
            ple_gate(2)
            splits(b, 31, 33)
            square_last(2)
            splits(b, 33, 36)
            act.wait_ge(gained, TT * 3)
            act.wait_ge(sumsq_done, 16 + 3)
            for t in range(TT):
                act.wait_ge(last_gate, t + 1)
                nc.scalar.activation(scratch[:, t, :], ple_banks[PLE_GROUPS[-1][3]][t][:, :], ACT.Sigmoid,
                                     scale=rstd[:, t:t + 1]).then_inc(sigmoid_done, 1)
                act.wait_ge(final_rows, t + 1)
                nc.scalar.activation(turn_bank[t][:, :], h[:, t, 3 * COLS:], ACT.Square,
                                     accum_out=sumsq[:, t, 3:4]).then_inc(final_squares, 1)
                act.wait_ge(gained, TT * 3 + t + 1)
                act.wait_ge(final_rstds, t + 1)
                for c in (0, 1):
                    nc.scalar.activation(h[:, t, COLS * c:COLS * (c + 1)], embedding[:, c, t, :], ACT.Copy,
                                         scale=rstd[:, t:t + 1]).then_inc(out_ready_act, 1)

        @block.vector
        def _(dve):
            chain = [0]

            def after_own(ins):
                chain[0] += 1
                ins.then_inc(dve_chain, 1)
                dve.wait_ge(dve_chain, chain[0])

            def split(blk, slot):
                dve.wait_ge(hi_split, blk + 1)
                nc.vector.tensor_tensor(w_lo[:, slot, :, :], raw[:, slot, :, :], w_hi[:, slot, :, :].bitcast(F32),
                                        ALU.subtract).then_inc(lo_split, 1)

            def splits(blk, j0, j1, slot0=None):
                for j in range(j0, j1):
                    split(blk + j, (blk + j) % RING if slot0 is None else (slot0 + j) % RING)

            def turn_gained(t, hi, lo, kt, gain):
                dve.wait_ge(turned_hi, t + 1)
                for k in range(2):
                    last = nc.vector.scalar_tensor_tensor(
                        out=lo[:, kt + k, :], in0=turn_bank[t % 2][:, k * TOK:(k + 1) * TOK],
                        scalar=gains[:, gain + kt + k:gain + kt + k + 1], in1=hi[:, kt + k, :].bitcast(F32),
                        op0=ALU.mult, op1=ALU.subtract)
                last.then_inc(turned_lo, 1)

            def turn_plain(t, bank, hi_ap, lo_ap):
                dve.wait_ge(turned_hi, t + 1)
                nc.vector.tensor_tensor(lo_ap, turn_bank[bank][:, :].rearrange("p (k c) -> p k c", k=2),
                                        hi_ap.bitcast(F32), ALU.subtract).then_inc(turned_lo, 1)

            def mean_square(n):
                dve.wait_ge(sumsq_done, 4 * n + 4)
                after_own(nc.vector.tensor_reduce(meansq[:], sumsq[:], AX_X, ALU.add))
                nc.vector.tensor_scalar(meansq[:], meansq[:], 1.0 / D, EPS, ALU.mult, ALU.add).then_inc(meansq_done, 1)

            silus = [0]

            def hidden_out(silu_count, bank):
                dve.wait_ge(silu_done, silu_count)
                for t in range(TT):
                    last = nc.vector.scalar_tensor_tensor(
                        out=scratch[:, t, TOK:], in0=acc[bank + t][:, TOK:], scalar=rstd[:, t:t + 1],
                        in1=scratch[:, t, 0:TOK], op0=ALU.mult, op1=ALU.mult)
                last.then_inc(read_out, 1)

            def turn_hidden(t, bank, group, kts):
                turn_plain(t, bank, slab_r[:, bass.ds(BK * group, BK), :], slab_r[:, bass.ds(kts + BK * group, BK), :])

            def up_groups(name, kts):
                b, n, t0, s0 = BLOCK[name], PHASES[name][0], TURN[name], silus[0]
                with dve.Fori(0, n // 2 - 1) as i:
                    for s in range(2):
                        start = b + 8 * (s + 1) + 16 * i
                        splits(start, 0, 4, 0)
                        hidden_out(s0 + s + 1 + 2 * i, 2 * s)
                        splits(start, 4, 6, 0)
                        turn_hidden(t0 + s + 2 * i, (t0 + s) % 2, s + 2 * i, kts)
                        splits(start, 6, 8, 0)
                start = b + 8 * (n - 1)
                splits(start, 0, 4)
                hidden_out(s0 + n - 1, 0)
                splits(start, 4, 6)
                turn_hidden(t0 + n - 2, (t0 + n) % 2, n - 2, kts)
                splits(start, 6, 8)
                silus[0] += n

            def rows_out(name, c, after, factor):
                dve.wait_ge(multiplied, after)
                for t in range(TT):
                    rows = h[:, t, COLS * c:COLS * (c + 1)]
                    last = nc.vector.scalar_tensor_tensor(out=rows, in0=acc[2 * (c % 2) + t][:, :], scalar=factor,
                                                          in1=rows, op0=ALU.mult, op1=ALU.add)
                last.then_inc(read_out, 1)

            def turn_rows(name, c, hi, lo, gain):
                for k in range(2):
                    turn_gained(TURN[name] + 2 * c + k, hi, lo, 4 * c + 2 * k, gain)

            def down_groups(up, down, kts, hi=None, lo=None, gain=None, turn_p=False):
                b, n, nb = BLOCK[down], PHASES[up][0], kts // BK
                for c in range(4):
                    start = b + nb * c
                    splits(start, 0, 4)
                    if c == 0:
                        hidden_out(silus[0], 2)
                    else:
                        rows_out(down, c - 1, start, 0.5)
                    splits(start, 4, 6)
                    if c == 0:
                        turn_hidden(TURN[up] + n - 1, (TURN[up] + n - 1) % 2, n - 1, kts)
                    elif gain is not None:
                        turn_rows(down, c - 1, hi, lo, gain)
                    splits(start, 6, nb)
                    if c == 0 and turn_p:
                        turn_plain(TURN["p"], TURN["p"] % 2, y_r[:, P_HI:P_HI + 2, :], y_r[:, P_LO:P_LO + 2, :])

            def second_part(up, down, before, hi, lo, gain, turn_p=False):
                b = BLOCK[up]
                splits(b, 0, 4)
                rows_out(before, 3, b, 0.5)
                splits(b, 4, 8)
                up_groups(up, HALF_KT[1])
                down_groups(up, down, HALF_KT[1], hi, lo, gain, turn_p)

            dve.wait_ge(gains_turned, 1)
            nc.vector.tensor_copy(gains[:, 0:KD], fox_bank[0][:, 0:KD]).then_inc(gains_ready, 1)
            dve.wait_ge(gains_ready, 1)
            b = BLOCK["up1a"]
            turn_gained(0, x_hi, x_lo, 0, 0)
            split(b, 0)
            for j in range(1, 8):
                split(b + j, j % RING)
                turn_gained(j, x_hi, x_lo, 2 * j, 0)
                if j == 4:
                    dve.wait_ge(gains_turned, 2)
                    nc.vector.tensor_copy(gains[:, KD:], fox_bank[1][:, KD:4 * KD + 2])
            mean_square(0)
            up_groups("up1a", HALF_KT[0])
            down_groups("up1a", "down1a", HALF_KT[0])
            second_part("up1b", "down1b", "down1a", x_hi, x_lo, KD)

            b = BLOCK["project"]
            splits(b, 0, 4)
            rows_out("down1b", 3, b, 0.5)
            splits(b, 4, 6)
            turn_rows("down1b", 3, x_hi, x_lo, KD)
            mean_square(1)
            splits(b, 6, 8)
            dve.wait_ge(thin_hi_done, 1)
            nc.vector.tensor_tensor(thin_w[:, :, P // 2:P // 2 + RANK], thin_raw[:, :, HEADS:THIN],
                                    thin_w[:, :, 0:RANK].bitcast(F32), ALU.subtract)
            fox_columns = slice(THIN_FOX, THIN_FOX + HEADS)
            fox_lo = slice(P // 2 + THIN_FOX, P // 2 + THIN_FOX + HEADS)
            nc.vector.tensor_tensor(thin_w[:, :, fox_lo], thin_raw[:, :, 0:HEADS], thin_w[:, :, fox_columns].bitcast(F32),
                                    ALU.subtract).then_inc(thin_lo_done, 1)
            with dve.Fori(1, 10) as i:
                splits(b + 8 * i, 0, 8, 0)
            start = b + 8 * 10
            dve.wait_ge(thin_turned, 1)
            dve.wait_ge(rstd_done, 2)
            for t in range(TT):
                last = nc.vector.tensor_scalar(thin_z[:, t, :], fox_bank[1][:, P * t:P * t + 2 * THIN_FOX], rstd[:, t:t + 1],
                                               None, ALU.mult)
            after_own(last)
            for t in range(TT):
                last = nc.vector.tensor_tensor(thin_z[:, t, fox_columns], thin_z[:, t, fox_columns], forget_bias[:], ALU.add)
            last.then_inc(thin_scaled, 1)
            dve.wait_ge(thin_scaled, 1)
            z = thin_z[:, :, fox_columns]
            nc.vector.scalar_tensor_tensor(out=thin_e[:], in0=z, scalar=-1.0, in1=z, op0=ALU.mult, op1=ALU.min)\
                .then_inc(thin_neg, 1)
            splits(start, 0, 3)
            dve.wait_ge(thin_log, 1)
            nc.vector.scalar_tensor_tensor(out=log_f[:], in0=z, scalar=0.0, in1=thin_e[:],
                                           op0=ALU.min, op1=ALU.subtract).then_inc(log_f_done, 1)
            splits(start, 3, 5)
            dve.wait_ge(down_turned, 1)
            nc.vector.tensor_copy(down_t[0:RANK, :], fox_bank[1][0:RANK, 2 * P:2 * P + TOK]).then_inc(down_ready, 1)
            splits(start, 5, 8)
            start += 8
            splits(start, 0, 1)
            dve.wait_ge(decay_log, 1)
            for t in range(TT):
                last = nc.vector.scalar_tensor_tensor(out=log_a[:, t, :], in0=turn_bank[t][:, :], scalar=0.0,
                                                      in1=log_a[:, t, :], op0=ALU.min, op1=ALU.subtract)
            last.then_inc(log_a_done, 1)
            splits(start, 1, 8)
            dve.wait_ge(suffix_exp, 1)
            for t in range(TT):
                keys = slab[:, GK:GK + GH, t, :]
                last = nc.vector.tensor_tensor(keys, keys, scratch[:, t, :].rearrange("p (s c) -> p s c", s=GH), ALU.mult)
            last.then_inc(k_decayed, 1)

            def merge_out(g, after):
                dve.wait_ge(multiplied, after)
                dve.wait_ge(bias_full[g % 2], 16 * (g // 2 + 1))
                for t in range(TT):
                    last = nc.vector.scalar_tensor_tensor(
                        out=gates[:, g, t, :], in0=acc[2 * (g % 2) + t][:, :], scalar=rstd[:, t:t + 1],
                        in1=merge_bias[:, g % 2, :], op0=ALU.mult, op1=ALU.add)
                last.then_inc(read_out, 1)

            def fox_mask_max(head):
                dve.wait_ge(fox_scored, head + 1)
                after_own(nc.vector.tensor_tensor(probs[:], fox_bank[1][:, 0:3 * P], causal[:], ALU.add))
                nc.vector.tensor_reduce(neg_max[:, 0:1], probs[:, 0:P], AX_X, ALU.max)
                after_own(nc.vector.tensor_reduce(neg_max[:, 1:2], probs[:, P:3 * P], AX_X, ALU.max))
                nc.vector.tensor_scalar(neg_max[:], neg_max[:], -1.0, None, ALU.mult).then_inc(fox_max, 1)

            def fox_normalise(head):
                dve.wait_ge(fox_exp, head + 1)
                after_own(nc.vector.reciprocal(row_inv[:], row_sum[:]))
                nc.vector.tensor_scalar(probs[:, 0:P], probs[:, 0:P], row_inv[:, 0:1], None, ALU.mult)
                nc.vector.tensor_scalar(probs[:, P:3 * P], probs[:, P:3 * P], row_inv[:, 1:2], None, ALU.mult)\
                    .then_inc(fox_probs, 1)

            def fox_result(head):
                dve.wait_ge(fox_y_hi, head + 1)
                nc.vector.tensor_tensor(slab_r[:, FK + head, :], fox_bank[1][:, 0:TOK],
                                        slab_r[:, FQ + head, :].bitcast(F32), ALU.subtract).then_inc(fox_y_lo, 1)

            def gla_update(g):
                pair, c = g // 4, g % 4
                dve.wait_ge(gla_kv, g + 1)
                for hh in range(2):
                    kv = turn_bank[0][:, hh * DV:(hh + 1) * DV]
                    if c == 0:
                        last = nc.vector.tensor_copy(state[:, hh, :], kv)
                    else:
                        at = (2 * pair + hh) * 4 + c
                        last = nc.vector.scalar_tensor_tensor(out=state[:, hh, :], in0=state[:, hh, :],
                                                              scalar=decay[:, at:at + 1], in1=kv,
                                                              op0=ALU.mult, op1=ALU.add)
                last.then_inc(gla_state, 1)

            def gla_mean(n):
                dve.wait_ge(gla_squares, n + 1)
                nc.vector.tensor_scalar(gla_meansq[:], gla_sumsq[:], 1.0 / DV, EPS, ALU.mult, ALU.add).then_inc(gla_means, 1)

            def gla_gate(n):
                pair, t = n // 2, n % 2
                dve.wait_ge(gla_rstds, n + 1)
                for hh in range(2):
                    s = GR + 2 * (2 * pair + hh)
                    last = nc.vector.scalar_tensor_tensor(
                        out=slab[:, s:s + 2, t, :], in0=turn_bank[1][:, hh * DV:(hh + 1) * DV].rearrange("p (d c) -> p d c", d=2),
                        scalar=gla_rstd[:, hh:hh + 1], in1=slab[:, s:s + 2, t, :], op0=ALU.mult, op1=ALU.mult)
                last.then_inc(gla_y, 1)

            def gla_result(n):
                pair, t = n // 2, n % 2
                dve.wait_ge(gla_y_hi, n + 1)
                turned_y = turn_bank[0][:, :].rearrange("p (h d c) -> p h d c", h=2, d=2)
                for d in range(2):
                    at, of = GV + 4 * pair + d, GR + 4 * pair + d
                    last = nc.vector.scalar_tensor_tensor(
                        out=slab_r[:, at:at + 3:2, t * P:(t + 1) * P], in0=turned_y[:, :, d, :],
                        scalar=gains[:, 4 * KD + d:4 * KD + d + 1],
                        in1=slab_r[:, of:of + 3:2, t * P:(t + 1) * P].bitcast(F32), op0=ALU.mult, op1=ALU.subtract)
                last.then_inc(gla_y_lo, 1)

            b = BLOCK["merge"]
            for g in range(8):
                start = b + 8 * g
                splits(start, 0, 1)
                if g in (3, 5, 7):
                    gla_result((g - 3) // 2)
                splits(start, 1, 2)
                if g > 0 and g % 2 == 0:
                    gla_mean(g // 2 - 1)
                splits(start, 2, 3)
                if g > 0 and g % 2 == 0:
                    gla_gate(g // 2 - 1)
                splits(start, 3, 4)
                if g > 0:
                    merge_out(g - 1, start)
                    fox_result(g - 1)
                splits(start, 4, 7)
                gla_update(g)
                fox_mask_max(g)
                splits(start, 7, 8)
                fox_normalise(g)

            def branch_a_out(c, after):
                dve.wait_ge(multiplied, after)
                dve.wait_ge(sigmoid_done, 2 * c + 1)
                for t in range(TT):
                    last = nc.vector.tensor_tensor(gates[:, c, t, :], acc[t][:, :], gates[:, c, t, :], ALU.mult)
                last.then_inc(read_out, 1)

            def branch_b_out(c, after):
                dve.wait_ge(multiplied, after)
                dve.wait_ge(sigmoid_done, 2 * c + 2)
                for t in range(TT):
                    last = nc.vector.tensor_tensor(gates[:, 4 + c, t, :], acc[2 + t][:, :], gates[:, 4 + c, t, :], ALU.mult)
                after_own(last)
                nc.vector.tensor_tensor(gates[:, c, :, :], gates[:, c, :, :], gates[:, 4 + c, :, :], ALU.add).then_inc(read_out, 1)

            def turn_merged(c):
                for k in range(2):
                    t, kt = TURN["branch"] + 2 * c + k, 4 * c + 2 * k
                    turn_plain(t, t % 2, x_hi[:, kt:kt + 2, :], x_lo[:, kt:kt + 2, :])

            b = BLOCK["branch"]
            for c in range(4):
                start = b + 8 * c
                splits(start, 0, 2)
                if c == 0:
                    gla_mean(3)
                splits(start, 2, 3)
                if c == 0:
                    gla_gate(3)
                splits(start, 3, 4)
                if c == 0:
                    merge_out(7, start)
                    fox_result(7)
                else:
                    branch_b_out(c - 1, start)
                splits(start, 4, 6)
                if c == 0:
                    gla_result(3)
                splits(start, 6, 7)
                if c > 0:
                    turn_merged(c - 1)
                splits(start, 7, 8)
                branch_a_out(c, start + 4)

            b = BLOCK["out"]
            for c in range(4):
                start = b + 8 * c
                splits(start, 0, 4)
                if c == 0:
                    branch_b_out(3, start)
                else:
                    rows_out("out", c - 1, start, 1.0)
                splits(start, 4, 6)
                if c > 0:
                    turn_rows("out", c - 1, y_r, y_r[:, KD:, :], 2 * KD)
                splits(start, 6, 7)
                if c == 0:
                    turn_merged(3)
                splits(start, 7, 8)

            b = BLOCK["up2a"]
            splits(b, 0, 4)
            rows_out("out", 3, b, 1.0)
            splits(b, 4, 6)
            turn_rows("out", 3, y_r, y_r[:, KD:, :], 2 * KD)
            mean_square(2)
            splits(b, 6, 8)
            dve.wait_ge(rstd_done, 3)
            up_groups("up2a", HALF_KT[0])
            down_groups("up2a", "down2a", HALF_KT[0])
            second_part("up2b", "down2b", "down2a", x_hi, x_lo, 3 * KD, True)

            def ple_out(c):
                dve.wait_ge(embedded, c + 1)
                columns = slice(COLS * c, COLS * (c + 1))
                for t in range(TT):
                    dve.wait_ge(sigmoid_done, 8 + TT * c + t + 1)
                    after_own(nc.vector.tensor_tensor(scratch[:, t, :], embedding[:, c, t, :], scratch[:, t, :], ALU.mult))
                    after_own(nc.vector.tensor_tensor(h[:, t, columns], h[:, t, columns], scratch[:, t, :], ALU.add))
                    nc.vector.tensor_tensor(embedding[:, c, t, :], h[:, t, columns], final_gain[:, columns], ALU.mult)\
                        .then_inc(gained, 1)

            b = BLOCK["ple"]
            splits(b, 0, 4)
            rows_out("down2b", 3, b, 0.5)
            splits(b, 4, 6)
            turn_rows("down2b", 3, x_hi, x_lo, 3 * KD)
            mean_square(3)
            splits(b, 6, 13)
            dve.wait_ge(tail_full, 32)
            ple_out(0)
            splits(b, 13, 22)
            ple_out(1)
            splits(b, 22, 31)
            ple_out(2)
            splits(b, 31, 36)
            for t in range(TT):
                rows = h[:, t, 3 * COLS:]
                dve.wait_ge(sigmoid_done, 8 + TT * 3 + t + 1)
                after_own(nc.vector.tensor_tensor(scratch[:, t, :], embedding[:, 3, t, :], scratch[:, t, :], ALU.mult))
                nc.vector.tensor_tensor(rows, rows, scratch[:, t, :], ALU.add).then_inc(final_rows, 1)
                dve.wait_ge(final_rows, t + 1)
                nc.vector.tensor_tensor(embedding[:, 3, t, :], rows, final_gain[:, 3 * COLS:], ALU.mult).then_inc(gained, 1)
                dve.wait_ge(final_squares, t + 1)
                after_own(nc.vector.tensor_reduce(meansq[:, t:t + 1], sumsq[:, t, :], AX_X, ALU.add))
                nc.vector.tensor_scalar(meansq[:, t:t + 1], meansq[:, t:t + 1], 1.0 / D, EPS, ALU.mult, ALU.add)\
                    .then_inc(final_means, 1)
                dve.wait_ge(final_rstds, t + 1)
                for c in (2, 3):
                    nc.vector.tensor_scalar(h[:, t, COLS * c:COLS * (c + 1)], embedding[:, c, t, :], rstd[:, t:t + 1],
                                            None, ALU.mult).then_inc(out_ready_dve, 1)

        @block.tensor
        def _(pe):
            def blocks(blk, bank, hi, lo, j0, j1, nb, slot0=None, tiles=None, banks=None):
                for j in range(j0, j1):
                    slot = (blk + j) % RING if slot0 is None else (slot0 + j) % RING
                    if tiles:
                        tiles(j)
                    pe.wait_ge(lo_split, blk + j + 1)
                    for k in range(BK):
                        kt = BK * j + k
                        for t in range(TT):
                            tok = slice(t * P, (t + 1) * P)
                            to = (banks or acc[bank:bank + TT])[t][:, :]
                            nc.tensor.matmul(to, hi(kt)[:, tok], w_hi[:, slot, k, :], start=kt == 0, stop=False)
                            nc.tensor.matmul(to, hi(kt)[:, tok], w_lo[:, slot, k, :], start=False, stop=False)
                            last = nc.tensor.matmul(to, lo(kt)[:, tok], w_hi[:, slot, k, :], start=False,
                                                    stop=kt == BK * nb - 1)
                    last.then_inc(multiplied, 1)

            def bank_free(group):
                pe.wait_ge(read_out, group - 1)

            def of(hi_tensor, lo_tensor, hi0=0, lo0=0):
                return (lambda kt: hi_tensor[:, hi0 + kt, :]), (lambda kt: lo_tensor[:, lo0 + kt, :])

            def turn(t, bank, tile):
                if not isinstance(t, int) or t >= 2:
                    pe.wait_ge(turned_lo, t - 1)
                for k in range(2):
                    for tok in range(TT):
                        at = k * TOK + tok * P
                        last = nc.tensor.transpose(turn_bank[bank][:, at:at + P], tile(k, tok), ident[:])
                last.then_inc(turned, 1)

            def turn_rows(name, c):
                pe.wait_ge(read_out, GROUP[name] + c + 1)
                for n in range(2):
                    t = TURN[name] + 2 * c + n
                    turn(t, t % 2, lambda k, tok: h[:, tok, (4 * c + 2 * n + k) * P:(4 * c + 2 * n + k + 1) * P])

            def turn_hidden(t, bank, group):
                pe.wait_ge(read_out, group)
                turn(t, bank, lambda k, tok: scratch[:, tok, TOK + k * P:TOK + (k + 1) * P])

            def tiles_of(first_turn):
                return lambda j: pe.wait_ge(turned_lo, first_turn + j + 1)

            def up_groups(name, hi, lo):
                b, n, t0, g = BLOCK[name], PHASES[name][0], TURN[name], GROUP[name]
                with pe.Fori(0, n // 2 - 1) as i:
                    for s in range(2):
                        start, group = b + 8 * (s + 1) + 16 * i, g + s + 1 + 2 * i
                        bank = 2 * ((s + 1) % 2)
                        bank_free(group)
                        blocks(start, bank, hi, lo, 0, 2, 8, 0)
                        turn_hidden(t0 + s + 2 * i, (t0 + s) % 2, group)
                        blocks(start, bank, hi, lo, 2, 8, 8, 0)
                start, group = b + 8 * (n - 1), g + n - 1
                bank_free(group)
                blocks(start, 2, hi, lo, 0, 2, 8)
                turn_hidden(t0 + n - 2, (t0 + n) % 2, group)
                blocks(start, 2, hi, lo, 2, 8, 8)

            def down_groups(up, down, kts, turns, turn_p=False):
                b, g, n, nb = BLOCK[down], GROUP[down], PHASES[up][0], kts // BK
                hi, lo = of(slab_r, slab_r, 0, kts)
                for c in range(4):
                    start, bank = b + nb * c, 2 * (c % 2)
                    bank_free(g + c)
                    tiles = tiles_of(TURN[up]) if c == 0 else None
                    blocks(start, bank, hi, lo, 0, 2, nb, tiles=tiles)
                    if c == 0:
                        turn_hidden(TURN[up] + n - 1, (TURN[up] + n - 1) % 2, g)
                    elif turns:
                        turn_rows(down, c - 1)
                    blocks(start, bank, hi, lo, 2, 6, nb, tiles=tiles)
                    if c == 0 and turn_p:
                        pe.wait_ge(tail_full, 32)
                        turn(TURN["p"], TURN["p"] % 2, lambda k, tok: p_tm[:, tok, k * P:(k + 1) * P])
                    blocks(start, bank, hi, lo, 6, nb, nb, tiles=tiles)

            pe.wait_ge(ident_ready, 1)
            pe.wait_ge(first_gains_full, 16)
            nc.tensor.transpose(fox_bank[0][:, 0:KD], gains_rows[0:KD, :], ident[0:KD, 0:KD]).then_inc(gains_turned, 1)

            def turn_x(n):
                pe.wait_ge(x_full[n], 16)
                turn(n, n % 2, lambda k, tok: h[:, tok, (2 * n + k) * P:(2 * n + k + 1) * P])

            x_of = of(x_hi, x_lo)
            turn_x(0)
            turn_x(1)
            for j in range(8):
                if j == 2:
                    pe.wait_ge(gains_full, 64)
                    nc.tensor.transpose(fox_bank[1][:, 0:4 * KD + 2], gains_rows[:], ident[0:4 * KD + 2, 0:4 * KD + 2])\
                        .then_inc(gains_turned, 1)
                blocks(0, 0, *x_of, j, j + 1, 8, tiles=tiles_of(0))
                if j + 2 < 8:
                    turn_x(j + 2)
            up_groups("up1a", *x_of)
            down_groups("up1a", "down1a", HALF_KT[0], False)
            bank_free(GROUP["up1b"])
            blocks(BLOCK["up1b"], 0, *x_of, 0, 8, 8)
            up_groups("up1b", *x_of)
            down_groups("up1b", "down1b", HALF_KT[1], True)

            b, g0 = BLOCK["project"], GROUP["project"]

            def after_rows(name, phase, hi_lo):
                start = BLOCK[phase]
                tiles = tiles_of(TURN[name])
                bank_free(GROUP[phase])
                blocks(start, 0, *hi_lo, 0, 2, 8, tiles=tiles)
                turn_rows(name, 3)
                blocks(start, 0, *hi_lo, 2, 8, 8, tiles=tiles)

            after_rows("down1b", "project", x_of)
            with pe.Fori(0, 4) as i:
                for s in range(2):
                    bank_free(g0 + s + 1 + 2 * i)
                    blocks(b + 8 * (s + 1) + 16 * i, 2 * ((s + 1) % 2), *x_of, 0, 8, 8, 0)
            start = b + 8 * 9
            bank_free(g0 + 9)
            blocks(start, 2, *x_of, 0, 1, 8)
            pe.wait_ge(thin_lo_done, 1)
            for kt in range(KD):
                to = fox_bank[0][:, 0:TOK]
                nc.tensor.matmul(to, thin_w[:, kt, :], x_hi[:, kt, :], start=kt == 0, stop=False)
                last = nc.tensor.matmul(to, thin_w[:, kt, :], x_lo[:, kt, :], start=False, stop=kt == KD - 1)
            last.then_inc(thin_mult, 1)
            blocks(start, 2, *x_of, 1, 4, 8)
            pe.wait_ge(thin_copied, 1)
            for t in range(TT):
                to, rows = fox_bank[1][:, t * P:t * P + P // 2], thin_rows[:, t * P:(t + 1) * P]
                nc.tensor.matmul(to, rows, ident[:, 0:P // 2], start=True, stop=False)
                last = nc.tensor.matmul(to, rows, ident[:, P // 2:P], start=False, stop=True)
            last.then_inc(thin_turned, 1)
            blocks(start, 2, *x_of, 4, 8, 8)
            start += 8
            bank_free(g0 + 10)
            blocks(start, 0, *x_of, 0, 1, 8)
            pe.wait_ge(thin_scaled, 1)
            for t in range(TT):
                last = nc.tensor.transpose(fox_bank[1][0:RANK, (2 + t) * P:(3 + t) * P], thin_z[:, t, 0:RANK], ident[:])
            last.then_inc(down_turned, 1)
            blocks(start, 0, *x_of, 1, 4, 8)
            pe.wait_ge(down_ready, 1)
            for t in range(TT):
                last = nc.tensor.matmul(turn_bank[t][:, :], down_t[0:RANK + 1, t * P:(t + 1) * P], gate_up, start=True, stop=True)
            last.then_inc(decay_mult, 1)
            blocks(start, 0, *x_of, 4, 8, 8)
            start += 8
            bank_free(g0 + 11)
            blocks(start, 2, *x_of, 0, 2, 8)
            pe.wait_ge(consts, 1)
            pe.wait_ge(log_a_done, 1)
            for t in range(TT):
                nc.tensor.matmul(fox_bank[t][:, :], later_in_chunk[:], log_a[:, t, :], start=True, stop=True)
            for hd in range(GH):
                for t in range(TT):
                    at = hd * 4 + 2 * t
                    last = nc.tensor.matmul(turn_bank[0][:, at:at + 2], log_a[:, t, hd * DK:(hd + 1) * DK], in_chunk[:],
                                            start=True, stop=True)
            last.then_inc(suffix_mult, 1)
            blocks(start, 2, *x_of, 2, 8, 8)

            def fox_turn(head):
                if head > 0:
                    pe.wait_ge(fox_probs_t, head)
                else:
                    pe.wait_ge(suffix_exp, 1)
                    pe.wait_ge(read_out, GROUP["project"] + 10)
                for n, s in enumerate((FQ + head, FK + head)):
                    for t in range(TT):
                        at = n * TOK + t * P
                        last = nc.tensor.transpose(fox_bank[0][:, at:at + P], slab[:, s, t, :], ident[:])
                last.then_inc(fox_turned, 1)

            def fox_scores(head):
                pe.wait_ge(fox_qk, head + 1)
                pe.wait_ge(fox_masked, 3 * head + 3)
                if head > 0:
                    pe.wait_ge(fox_y_lo, head)
                m = masked_log_f[:, head % 2, :, :]
                s0, s1 = fox_bank[1][:, 0:P], fox_bank[1][:, P:3 * P]
                nc.tensor.matmul(s0, qk_t[:, 0:P], qk_t[:, TOK:TOK + P], start=True, stop=False)
                nc.tensor.matmul(s0, m[:, 0, :], behind[:, 0, 0:P], start=False, stop=True)
                nc.tensor.matmul(s1, qk_t[:, P:TOK], qk_t[:, TOK:], start=True, stop=False)
                nc.tensor.matmul(fox_bank[1][:, P:2 * P], m[:, 1, :], behind[:, 0, 0:P], start=False, stop=False)
                nc.tensor.matmul(s1, m[:, 2, :], behind[:, 1, :], start=False, stop=True).then_inc(fox_scored, 1)

            def fox_turn_probs(head):
                pe.wait_ge(fox_probs, head + 1)
                for n in range(3):
                    last = nc.tensor.transpose(fox_bank[0][:, n * P:(n + 1) * P], probs[:, n * P:(n + 1) * P], ident[:])
                last.then_inc(fox_probs_turned, 1)

            def fox_mix(head):
                pe.wait_ge(fox_probs_t, head + 1)
                nc.tensor.matmul(fox_bank[1][:, 0:TOK], slab[:, FV + head, 0, :], probs_t[:, 0:TOK],
                                 start=True, stop=False, skip_group_check=True)
                nc.tensor.matmul(fox_bank[1][:, P:TOK], slab[:, FV + head, 1, :], probs_t[:, TOK:],
                                 start=False, stop=True, skip_group_check=True).then_inc(fox_mixed, 1)

            def gla_turn_queries(pair):
                if pair > 0:
                    pe.wait_ge(gla_state, 4)
                for hh in range(2):
                    for t in range(TT):
                        at = hh * TOK + t * P
                        last = nc.tensor.transpose(turn_bank[0][:, at:at + P], slab[:, GQ + 2 * pair + hh, t, :], ident[:])
                last.then_inc(gla_q_turned, 1)

            def gla_products(g):
                pair, c = g // 4, g % 4
                rows, t = chunk_rows(c)
                pe.wait_ge(gla_q_ready, pair + 1)
                pe.wait_ge(k_decayed, 1)
                if g > 0:
                    pe.wait_ge(gla_state, g)
                if g >= 3:
                    pe.wait_ge(gla_y_lo, (g - 1) // 2)
                for hh in range(2):
                    hd = 2 * pair + hh
                    last = nc.tensor.matmul(turn_bank[0][:, hh * DV:(hh + 1) * DV], slab[rows, GK + hd, t, :],
                                            slab[rows, GV + 2 * hd:GV + 2 * hd + 2, t, :], start=True, stop=True)
                last.then_inc(gla_kv, 1)

            def gla_read_state(g):
                c = g % 4
                rows, t = chunk_rows(c)
                pe.wait_ge(gla_state, g + 1)
                if g >= 2 and c % 2 == 0:
                    pe.wait_ge(gla_y, g // 2)
                for hh in range(2):
                    at = t * P + rows.start
                    last = nc.tensor.matmul(turn_bank[1][rows, hh * DV:(hh + 1) * DV], gq_t[:, hh, at:at + CHUNK],
                                            state[:, hh, :], start=True, stop=True)
                last.then_inc(gla_read, 1)

            def gla_turn_result(n):
                pair, t = n // 2, n % 2
                pe.wait_ge(gla_y, n + 1)
                pe.wait_ge(gla_state, min(2 * n + 3, 8))
                for hh in range(2):
                    for d in range(2):
                        at = (2 * hh + d) * P
                        last = nc.tensor.transpose(turn_bank[0][:, at:at + P], slab[:, GR + 4 * pair + 2 * hh + d, t, :], ident[:])
                last.then_inc(gla_y_turned, 1)

            b, g0 = BLOCK["merge"], GROUP["merge"]
            for g in range(8):
                start, bank = b + 8 * g, 2 * (g % 2)
                bank_free(g0 + g)
                blocks(start, bank, *x_of, 0, 1, 8)
                fox_turn(g)
                if g % 4 == 0:
                    gla_turn_queries(g // 4)
                blocks(start, bank, *x_of, 1, 3, 8)
                fox_scores(g)
                gla_products(g)
                blocks(start, bank, *x_of, 3, 5, 8)
                if g > 0 and g % 2 == 0:
                    gla_turn_result(g // 2 - 1)
                blocks(start, bank, *x_of, 5, 6, 8)
                fox_turn_probs(g)
                gla_read_state(g)
                blocks(start, bank, *x_of, 6, 8, 8)
                fox_mix(g)

            b, g0 = BLOCK["branch"], GROUP["branch"]
            fox_of, gla_of = of(slab_r, slab_r, FQ, FK), of(slab_r, slab_r, GR, GV)

            def turn_merged(c):
                pe.wait_ge(read_out, g0 + 2 * c + 2)
                for n in range(2):
                    t = TURN["branch"] + 2 * c + n
                    turn(t, t % 2, lambda k, tok: gates[:, c, tok, (2 * n + k) * P:(2 * n + k + 1) * P])

            for c in range(4):
                start = b + 8 * c
                bank_free(g0 + 2 * c)
                tiles = (lambda j: pe.wait_ge(fox_y_lo, 2 * j + 2)) if c == 0 else None
                blocks(start, 0, *fox_of, 0, 2, 4, tiles=tiles)
                if c == 0:
                    gla_turn_result(3)
                blocks(start, 0, *fox_of, 2, 3, 4, tiles=tiles)
                if c == 1:
                    pe.wait_ge(gla_y_lo, 4)
                if c > 0:
                    turn_merged(c - 1)
                blocks(start, 0, *fox_of, 3, 4, 4, tiles=tiles)
                bank_free(g0 + 2 * c + 1)
                tiles = (lambda j: pe.wait_ge(gla_y_lo, 2 if j < 2 else 4)) if c == 0 else None
                blocks(start + 4, 2, *gla_of, 0, 4, 4, tiles=tiles)

            b, g0o = BLOCK["out"], GROUP["out"]
            for c in range(4):
                start, bank = b + 8 * c, 2 * (c % 2)
                bank_free(g0o + c)
                tiles = tiles_of(TURN["branch"]) if c == 0 else None
                blocks(start, bank, *x_of, 0, 2, 8, tiles=tiles)
                if c > 0:
                    turn_rows("out", c - 1)
                blocks(start, bank, *x_of, 2, 3, 8, tiles=tiles)
                if c == 0:
                    turn_merged(3)
                blocks(start, bank, *x_of, 3, 8, 8, tiles=tiles)

            y_of = of(y_r, y_r, 0, KD)
            after_rows("out", "up2a", y_of)
            up_groups("up2a", *y_of)
            down_groups("up2a", "down2a", HALF_KT[0], False)
            bank_free(GROUP["up2b"])
            blocks(BLOCK["up2b"], 0, *y_of, 0, 8, 8)
            up_groups("up2b", *y_of)
            down_groups("up2b", "down2b", HALF_KT[1], True, True)

            p_of = of(y_r, y_r, P_HI, P_LO)
            for kind, c, first, banks in PLE_GROUPS:
                start, at = BLOCK["ple"] + first, ple_banks[banks]
                if kind == "E":
                    if c == 0:
                        pe.wait_ge(turned_lo, TURN["p"] + 1)
                        bank_free(GROUP["ple"])
                    elif c > 1:
                        pe.wait_ge(embedded, c)
                    blocks(start, 0, *p_of, 0, 1, 1, banks=at)
                    if c == 1:
                        turn_rows("down2b", 3)
                else:
                    if c == 1:
                        pe.wait_ge(embedded, 1)
                    if c > 1:
                        pe.wait_ge(sigmoid_done, 8 + TT * (c - 1))
                    blocks(start, 0, *x_of, 0, 8 if c < 3 else 4, 8, tiles=tiles_of(TURN["down2b"]) if c == 0 else None,
                           banks=at)
            for t in range(TT):
                tok = slice(t * P, (t + 1) * P)
                for blk in range(END - RING, END):
                    pe.wait_ge(lo_split, blk + 1)
                    for k in range(BK):
                        kt, slot = KD - BK * (END - blk) + k, blk % RING
                        nc.tensor.matmul(at[t][:, :], x_hi[:, kt, tok], w_hi[:, slot, k, :], start=False, stop=False)
                        nc.tensor.matmul(at[t][:, :], x_hi[:, kt, tok], w_lo[:, slot, k, :], start=False, stop=False)
                        last = nc.tensor.matmul(at[t][:, :], x_lo[:, kt, tok], w_hi[:, slot, k, :], start=False,
                                                stop=kt == KD - 1)
                last.then_inc(last_gate, 1)


_INS = ["x", "p", "ffn1_norm", "ffn1_w_gate", "ffn1_w_up", "ffn1_w_down", "mix_norm", "w_in",
        "fox_forget_bias", "gla_gate_up", "gla_gate_bias", "gla_head_norm", "w_branch_fox",
        "w_branch_gla", "w_merge_gate", "b_merge_gate", "w_out", "ffn2_norm", "ffn2_w_gate",
        "ffn2_w_up", "ffn2_w_down", "ple_norm", "w_ple_proj", "w_ple_gate", "final_norm"]


def kernel(**inputs):
    import numpy as np
    import concourse.bacc as bacc
    from concourse.bass_utils import run_bass_kernel_spmd

    nc = bacc.Bacc("TRN2", target_bir_lowering=False, num_devices=1)
    arrays, args = {}, []
    for name in _INS:
        a = np.ascontiguousarray(inputs[name])
        arrays[f"in_{name}"] = a
        args.append(nc.dram_tensor(f"in_{name}", a.shape, mybir.dt.from_np(a.dtype), kind="ExternalInput").ap())
    args.append(nc.dram_tensor("out_0", (1, TOK, D), F32, kind="ExternalOutput").ap())
    build(nc, *args)
    r = run_bass_kernel_spmd(nc, [arrays], core_ids=[0])
    return r.results[0]["out_0"]
```
